# Optimizing a Trainium2 kernel written in Bass

```python
import math
import jax
import jax.numpy as jnp
from jax import lax
import numpy as np

D_MODEL = 1024
BATCH = 1
SEQ = 128
DEPTH = 1
DEC_BATCH = 1
DEC_SEQ = 512
PAST_LEN = 128

GRID_W = 64
RMS_EPS = 1e-6
S5_WIDTH = D_MODEL // 2
S5_GROUP = 16
S5_GROUPS = S5_WIDTH // S5_GROUP
S5_STATE = 64
HG_HEADS = 4
HG_DK = 128
HG_DV = (D_MODEL // 2) // HG_HEADS
HG_WIDTH = HG_HEADS * HG_DV
HG_KW = HG_HEADS * HG_DK
HG_CHUNK = 64
N_EXPERTS = 16
N_GROUPS = 4
EXPERTS_PER_GROUP = N_EXPERTS // N_GROUPS
TOP_K = 2
D_FF = D_MODEL
MOE_BLOCK = 128
IN_COLS = S5_WIDTH + 3 * HG_KW + 2 * HG_WIDTH + 2 * D_MODEL
IN_SPLITS = (S5_WIDTH, S5_WIDTH + HG_KW, S5_WIDTH + 2 * HG_KW, S5_WIDTH + 3 * HG_KW,
             S5_WIDTH + 3 * HG_KW + HG_WIDTH, S5_WIDTH + 3 * HG_KW + 2 * HG_WIDTH,
             S5_WIDTH + 3 * HG_KW + 2 * HG_WIDTH + D_MODEL)

kernel_name = 'hybrid_s5_hgrn2_moe_diffusion_step'

def rmsnorm(x, w):
    xf = x.astype(jnp.float32)
    y = xf * lax.rsqrt(jnp.mean(xf * xf, axis=-1, keepdims=True) + RMS_EPS)
    return y.astype(x.dtype) * w

def adaln(cvec, w_ada, b_ada):
    m = jax.nn.silu(cvec) @ w_ada + b_ada
    return jnp.split(m[:, None, :], 6, axis=-1)

def grid_pos_embed(rows, dtype):
    f32 = jnp.float32
    r = jnp.repeat(jnp.arange(rows, dtype=f32), GRID_W)
    col = jnp.tile(jnp.arange(GRID_W, dtype=f32), rows)
    quarter = D_MODEL // 4
    omega = 1.0 / (10000.0 ** (jnp.arange(quarter, dtype=f32) / quarter))

    def axis_embed(p):
        ang = p[:, None] * omega[None, :]
        return jnp.concatenate([jnp.sin(ang), jnp.cos(ang)], axis=-1)

    return jnp.concatenate([axis_embed(r), axis_embed(col)], axis=-1).astype(dtype)

def s5_scan(bu, lam_bar):
    a = jnp.broadcast_to(lam_bar, bu.shape)

    def combine(e1, e2):
        a1, b1 = e1
        a2, b2 = e2
        return a1 * a2, a2 * b1 + b2

    return lax.associative_scan(combine, (a, bu), axis=1)[1]

def s5_mixer(u, h0, lam_re, lam_im, log_step, b_re, b_im, c_re, c_im, s5_d, w_glu, b_glu):
    f32 = jnp.float32
    bsz, L, _ = u.shape
    uf = u.astype(f32).reshape(bsz, L, S5_GROUPS, S5_GROUP)
    uc = uf.astype(jnp.complex64)
    b_c = lax.complex(b_re.astype(f32), b_im.astype(f32))
    c_c = lax.complex(c_re.astype(f32), c_im.astype(f32))
    total = None
    finals = []
    for d in range(2):
        lam = lax.complex(jnp.minimum(lam_re[d].astype(f32), -1e-4), lam_im[d].astype(f32))
        step = jnp.exp(log_step[d].astype(f32))[:, None]
        lam_bar = jnp.exp(lam * step)
        b_bar = ((lam_bar - 1.0) / lam)[:, :, None] * b_c
        ud = uc if d == 0 else uc[:, ::-1]
        bu = jnp.einsum('blgc,gpc->blgp', ud, b_bar)
        if h0 is not None:
            bu = bu.at[:, 0].add(lam_bar * h0[:, d])
        st = s5_scan(bu, lam_bar)
        finals.append(st[:, -1])
        st = st if d == 0 else st[:, ::-1]
        total = st if total is None else total + st
    y = jnp.einsum('gcp,blgp->blgc', c_c, total).real + s5_d.astype(f32) * uf
    g = jax.nn.gelu(y.reshape(bsz, L, S5_WIDTH))
    out = g * jax.nn.sigmoid(g @ w_glu.astype(f32) + b_glu.astype(f32))
    return out.astype(u.dtype), jnp.stack(finals, axis=1)

def gla_chunked(q, k, v, logf, h0):
    bsz, L, H, _ = q.shape
    dv = v.shape[-1]
    n = L // HG_CHUNK

    def chunks(t):
        return t.reshape(bsz, n, HG_CHUNK, H, t.shape[-1]).transpose(1, 0, 3, 2, 4)

    tri = jnp.tril(jnp.ones((HG_CHUNK, HG_CHUNK), dtype=bool))[:, :, None]

    def step(S, blk):
        qb, kb, vb, gb = blk
        bcum = jnp.cumsum(gb, axis=2)
        rel = bcum[:, :, :, None, :] - bcum[:, :, None, :, :]
        decay = jnp.exp(jnp.where(tri, rel, -jnp.inf))
        att = jnp.einsum('bhtd,bhsd,bhtsd->bhts', qb, kb, decay)
        o = jnp.einsum('bhts,bhsv->bhtv', att, vb) + jnp.einsum('bhtd,bhdv->bhtv', qb * jnp.exp(bcum), S)
        btot = bcum[:, :, -1:]
        S = S * jnp.exp(btot[:, :, 0])[..., None] + jnp.einsum('bhsd,bhsv->bhdv', kb * jnp.exp(btot - bcum), vb)
        return S, o

    S, o = lax.scan(step, h0, (chunks(q), chunks(k), chunks(v), chunks(logf)))
    return o.transpose(1, 0, 3, 2, 4).reshape(bsz, L, H, dv), S

def hgrn2_mixer(q_in, f_fwd, f_bwd, i_in, g_out, h0, lb, norm_w):
    f32 = jnp.float32
    bsz, L, _ = q_in.shape
    q = jax.nn.silu(q_in.astype(f32).reshape(bsz, L, HG_HEADS, HG_DK)) * (HG_DK ** -0.5)
    v = i_in.astype(f32).reshape(bsz, L, HG_HEADS, HG_DV)
    total = None
    finals = []
    for d, f_raw in enumerate((f_fwd, f_bwd)):
        f = lb[d] + (1.0 - lb[d]) * jax.nn.sigmoid(f_raw.astype(f32))
        f = f.reshape(bsz, L, HG_HEADS, HG_DK)
        k, logf = 1.0 - f, jnp.log(f)
        args = (q, k, v, logf) if d == 0 else (q[:, ::-1], k[:, ::-1], v[:, ::-1], logf[:, ::-1])
        s0 = jnp.zeros((bsz, HG_HEADS, HG_DK, HG_DV), f32) if h0 is None else h0[:, d]
        o, S = gla_chunked(*args, s0)
        finals.append(S)
        o = o if d == 0 else o[:, ::-1]
        total = o if total is None else total + o
    o = total * lax.rsqrt(jnp.mean(total * total, axis=-1, keepdims=True) + RMS_EPS)
    o = o.reshape(bsz, L, HG_WIDTH) * norm_w.astype(f32) * jax.nn.silu(g_out.astype(f32))
    return o.astype(q_in.dtype), jnp.stack(finals, axis=1)

def moe_ffn(x, router_w, router_b, w_gate, w_up, w_down):
    f32 = jnp.float32
    n_tok, dm = x.shape
    scores = jax.nn.sigmoid(x.astype(f32) @ router_w.astype(f32))
    sel = (scores + router_b.astype(f32)).reshape(n_tok, N_GROUPS, EXPERTS_PER_GROUP)
    group_score = lax.top_k(sel, 2)[0].sum(-1)
    best = jnp.argmax(group_score, axis=-1)
    in_group = jnp.take_along_axis(sel, best[:, None, None], axis=1)[:, 0]
    _, local = lax.top_k(in_group, TOP_K)
    expert = best[:, None] * EXPERTS_PER_GROUP + local
    wts = jnp.take_along_axis(scores, expert, axis=1)
    wts = wts / jnp.sum(wts, axis=-1, keepdims=True)
    n_slots = n_tok * TOP_K
    flat_e = expert.reshape(-1)
    order = jnp.argsort(flat_e)
    e_sorted = flat_e[order]
    counts = jnp.zeros((N_EXPERTS,), jnp.int32).at[flat_e].add(1)
    padded = (counts + MOE_BLOCK - 1) // MOE_BLOCK * MOE_BLOCK
    pad_end = jnp.cumsum(padded)
    pad_start = pad_end - padded
    raw_start = jnp.cumsum(counts) - counts
    dest = pad_start[e_sorted] + jnp.arange(n_slots, dtype=jnp.int32) - raw_start[e_sorted]
    n_blocks = -(-n_slots // MOE_BLOCK) + N_EXPERTS
    tok = order // TOP_K
    xb = jnp.zeros((n_blocks * MOE_BLOCK, dm), x.dtype).at[dest].set(x[tok])
    blk_expert = jnp.minimum(
        jnp.searchsorted(pad_end, jnp.arange(n_blocks, dtype=jnp.int32) * MOE_BLOCK, side='right'),
        N_EXPERTS - 1)

    def expert_block(args):
        xe, e = args
        return (jax.nn.silu(xe @ w_gate[e]) * (xe @ w_up[e])) @ w_down[e]

    yb = lax.map(expert_block, (xb.reshape(n_blocks, MOE_BLOCK, dm), blk_expert)).reshape(-1, dm)
    y_slot = yb[dest] * wts.reshape(-1)[order][:, None].astype(x.dtype)
    return jax.ops.segment_sum(y_slot, tok, num_segments=n_tok)

def trunk_layer(x, cvec, s5_h0, hg_h0, lb, w_ada, b_ada, norm1_w, norm2_w, w_in,
                lam_re, lam_im, log_step, b_re, b_im, c_re, c_im, s5_d, w_glu, b_glu,
                hg_norm_w, w_br_s5, w_br_hg, w_out, router_w, router_b, w_gate, w_up, w_down):
    shift1, scale1, gate1, shift2, scale2, gate2 = adaln(cvec, w_ada, b_ada)
    h = rmsnorm(x, norm1_w) * (1.0 + scale1) + shift1
    u, q_in, f_fwd, f_bwd, i_in, g_out, gate_s5, gate_hg = jnp.split(h @ w_in, IN_SPLITS, axis=-1)
    y_s5, s5_fin = s5_mixer(u, s5_h0, lam_re, lam_im, log_step, b_re, b_im, c_re, c_im, s5_d, w_glu, b_glu)
    y_hg, hg_fin = hgrn2_mixer(q_in, f_fwd, f_bwd, i_in, g_out, hg_h0, lb, hg_norm_w)
    merged = jax.nn.sigmoid(gate_s5) * (y_s5 @ w_br_s5) + jax.nn.sigmoid(gate_hg) * (y_hg @ w_br_hg)
    x = x + gate1 * (merged @ w_out)
    h = rmsnorm(x, norm2_w) * (1.0 + scale2) + shift2
    bsz, L, _ = x.shape
    ffn = moe_ffn(h.reshape(bsz * L, D_MODEL), router_w, router_b, w_gate, w_up, w_down)
    x = x + gate2 * ffn.reshape(bsz, L, D_MODEL)
    return x, s5_fin, hg_fin

def setup_inputs(seed: int = 0) -> dict:
    key = jax.random.key(seed)
    ks = iter(jax.random.split(key, 40))
    f32 = jnp.float32

    def nrm(shape, scale):
        return scale * jax.random.normal(next(ks), shape, f32)

    G, P = S5_GROUPS, S5_STATE
    n_idx = jnp.arange(P, dtype=f32)
    return {
        'x_prompt': nrm((BATCH, SEQ, D_MODEL), 1.0),
        'x_sample': nrm((DEC_BATCH, DEC_SEQ, D_MODEL), 1.0),
        'state_s5_re': nrm((DEC_BATCH, DEPTH, 2, G, P), 0.3),
        'state_s5_im': nrm((DEC_BATCH, DEPTH, 2, G, P), 0.3),
        'state_hg': nrm((DEC_BATCH, DEPTH, 2, HG_HEADS, HG_DK, HG_DV), 0.3),
        'c': nrm((DEC_BATCH, D_MODEL), 1.0),
        'c_ctx': nrm((D_MODEL,), 1.0),
        'w_ada': nrm((DEPTH, D_MODEL, 6 * D_MODEL), 0.5 * D_MODEL ** -0.5),
        'b_ada': nrm((DEPTH, 6 * D_MODEL), 0.01),
        'norm1_w': 1.0 + nrm((DEPTH, D_MODEL), 0.01),
        'norm2_w': 1.0 + nrm((DEPTH, D_MODEL), 0.01),
        'w_in': nrm((DEPTH, D_MODEL, IN_COLS), D_MODEL ** -0.5),
        's5_lam_re': -0.5 + nrm((DEPTH, 2, G, P), 0.01),
        's5_lam_im': math.pi * n_idx + nrm((DEPTH, 2, G, P), 0.01),
        's5_log_step': jax.random.uniform(next(ks), (DEPTH, 2, G), f32, math.log(1e-3), math.log(1e-1)),
        's5_b_re': nrm((DEPTH, G, P, S5_GROUP), (2 * S5_GROUP) ** -0.5),
        's5_b_im': nrm((DEPTH, G, P, S5_GROUP), (2 * S5_GROUP) ** -0.5),
        's5_c_re': nrm((DEPTH, G, S5_GROUP, P), (2 * P) ** -0.5),
        's5_c_im': nrm((DEPTH, G, S5_GROUP, P), (2 * P) ** -0.5),
        's5_d': nrm((DEPTH, G, S5_GROUP), 0.5),
        's5_w_glu': nrm((DEPTH, S5_WIDTH, S5_WIDTH), S5_WIDTH ** -0.5),
        's5_b_glu': nrm((DEPTH, S5_WIDTH), 0.01),
        'hg_lb_logits': nrm((DEPTH, 2, HG_KW), 0.1),
        'hg_norm_w': 1.0 + nrm((DEPTH, HG_WIDTH), 0.01),
        'w_br_s5': nrm((DEPTH, S5_WIDTH, D_MODEL), S5_WIDTH ** -0.5),
        'w_br_hg': nrm((DEPTH, HG_WIDTH, D_MODEL), HG_WIDTH ** -0.5),
        'w_out': nrm((DEPTH, D_MODEL, D_MODEL), D_MODEL ** -0.5),
        'router_w': nrm((D_MODEL, N_EXPERTS), D_MODEL ** -0.5),
        'router_b': nrm((N_EXPERTS,), 0.01),
        'moe_w_gate': nrm((DEPTH, N_EXPERTS, D_MODEL, D_FF), D_MODEL ** -0.5),
        'moe_w_up': nrm((DEPTH, N_EXPERTS, D_MODEL, D_FF), D_MODEL ** -0.5),
        'moe_w_down': nrm((DEPTH, N_EXPERTS, D_FF, D_MODEL), D_FF ** -0.5),
        'norm_f_w': 1.0 + nrm((D_MODEL,), 0.01),
    }

def reference(x_prompt, x_sample, state_s5_re, state_s5_im, state_hg, c, c_ctx, w_ada, b_ada,
              norm1_w, norm2_w, w_in, s5_lam_re, s5_lam_im, s5_log_step, s5_b_re, s5_b_im,
              s5_c_re, s5_c_im, s5_d, s5_w_glu, s5_b_glu, hg_lb_logits, hg_norm_w, w_br_s5,
              w_br_hg, w_out, router_w, router_b, moe_w_gate, moe_w_up, moe_w_down, norm_f_w):
    f32 = jnp.float32
    probs = jax.nn.softmax(hg_lb_logits.astype(f32), axis=0)
    lower_bounds = jnp.cumsum(probs, axis=0) - probs[0]
    rows = x_sample.shape[1] // GRID_W
    xs = x_sample + grid_pos_embed(rows, x_sample.dtype)[None]
    xp = x_prompt
    new_s5, new_hg = [], []
    for l in range(DEPTH):
        lw = (lower_bounds[l], w_ada[l], b_ada[l], norm1_w[l], norm2_w[l], w_in[l],
              s5_lam_re[l], s5_lam_im[l], s5_log_step[l], s5_b_re[l], s5_b_im[l], s5_c_re[l], s5_c_im[l],
              s5_d[l], s5_w_glu[l], s5_b_glu[l], hg_norm_w[l], w_br_s5[l], w_br_hg[l], w_out[l],
              router_w, router_b, moe_w_gate[l], moe_w_up[l], moe_w_down[l])
        xp, s5_fin, hg_fin = trunk_layer(xp, c_ctx[None], None, None, *lw)
        new_s5.append(s5_fin)
        new_hg.append(hg_fin)
        s5_h0 = lax.complex(state_s5_re[:, l].astype(f32), state_s5_im[:, l].astype(f32))
        xs, _, _ = trunk_layer(xs, c, s5_h0, state_hg[:, l].astype(f32), *lw)
    y_prompt = rmsnorm(xp, norm_f_w)
    y_sample = rmsnorm(xs, norm_f_w)
    s5_all = jnp.stack(new_s5, axis=1)
    new_state_s5_re = s5_all.real.astype(state_s5_re.dtype)
    new_state_s5_im = s5_all.imag.astype(state_s5_im.dtype)
    new_state_hg = jnp.stack(new_hg, axis=1).astype(state_hg.dtype)
    return (y_prompt, y_sample, new_state_s5_re, new_state_s5_im, new_state_hg)


_drawn_inputs = setup_inputs


def setup_inputs(seed=0):
    import zlib

    import numpy as np

    out = dict(_drawn_inputs(seed))
    spreads = {}
    factors = {'state_s5_re': 4.221,
     'state_s5_im': 3.894,
     'state_hg': 25.378,
     'b_ada': 2.894,
     'norm1_w': 5.432,
     'norm2_w': 3.853,
     's5_lam_re': 23.486,
     's5_c_re': 4.122,
     's5_c_im': 4.676,
     's5_w_glu': 3.43,
     's5_b_glu': 8.0,
     'hg_norm_w': 8.0,
     'norm_f_w': 29.385}
    for name, (base, spread) in spreads.items():
        noise = np.random.default_rng([zlib.crc32(name.encode()), seed]).standard_normal(out[name].shape)
        drawn = base * np.exp(spread * noise) if base else spread * noise
        out[name] = jnp.asarray(drawn.astype(out[name].dtype))
    for name, factor in factors.items():
        out[name] = (out[name] * factor).astype(out[name].dtype)
    return out
```

```python
import numpy as np
import concourse.bass as bass
from concourse import mybir
from contextlib import ExitStack

F32 = mybir.dt.float32
I32 = mybir.dt.int32
U8 = mybir.dt.uint8
ALU = mybir.AluOpType
ACT = mybir.ActivationFunctionType
AX = mybir.AxisListType

P = 128
D = 1024
KD = D // P
SAMPLE = 512
PROMPT = 128
TOK = SAMPLE + PROMPT
HALF = TOK // 2
CH = TOK // P
SCH = SAMPLE // P
EPS = 1e-6
BLK = 8
NB = TOK // BLK
SB = SAMPLE // BLK
PB = PROMPT // BLK
GROUPS, STATE, GC = 32, 64, 16
PAIRS = GROUPS // 2
SLOT = 2 * 2 * PAIRS
KW = (2 * BLK - 1) * GC
TWO_PI = 6.283185307179586
MAGIC = 12582912.0
HEADS = 4
LEVELS = 7
TINY = 2.0 ** -60
EXPERTS, EGROUPS, EPG = 16, 4, 4
OVER = 9
NBLK = EXPERTS + OVER
DFF = 1024
KF = DFF // P
T_ADA1, T_U, T_Q, T_FF, T_FB, T_V, T_ADA2, T_GLU, T_ADA3, T_G, T_MERGE = 0, 16, 20, 24, 28, 32, 36, 54, 56, 70, 74
TILES = T_MERGE + 3 * KD
RING = 6
ADA_MID = T_GLU - T_ADA2
ADA_Y = 16

SMALL = {}
_at = 0
for _name, _n in (("lam_re", 32), ("lam_im", 32), ("log_step", 32), ("b_re", 256), ("b_im", 256), ("c_re", 256),
                  ("c_im", 256), ("h0", 64), ("cvec", 16), ("b_ada", 48), ("norm1", 8), ("norm2", 8),
                  ("lb_logits", 8), ("hg_norm", 4), ("b_glu", 4), ("s5_d", 8), ("router_b", 16),
                  ("pos_row", 32), ("pos_col", 256), ("id16", 16), ("count", 32)):
    SMALL[_name] = (_at, _n)
    _at += _n
SMALL_COLS = _at
CONST = {"ident": (0, 128), "ones": (128, 128), "before": (256, 128), "reset_f": (384, 640), "reset_b": (1024, 640),
         "lower": (1664, 16), "eps": (1680, 1)}
CONST_COLS = 1696


def hybrid_step(nc, x_t, x_rows, pos_rows, small, const, masks, stream, w_out, norm_f, hg_state, router_w,
                w_gate, w_up, w_down, y_rows, s5_new, hg_new):
    ctx = ExitStack()
    with ctx:
        def sem(name):
            return ctx.enter_context(nc.semaphore(name))

        base = nc.sbuf_base
        base = (base + 63) // 64 * 64

        def at(name, offset, shape, dt=F32):
            return nc.alloc_sbuf_tensor_at(name, shape, dt, offset=base + offset)

        top = [0]

        def put(name, shape, dt=F32):
            size = 4 if dt != U8 else 1
            for n in shape[1:]:
                size *= n
            here = top[0]
            top[0] = (here + size + 63) // 64 * 64
            return at(name, here, shape, dt)

        sm = put("small_params", [P, SMALL_COLS])
        cst = put("constants", [P, CONST_COLS])
        mask = put("masks", [P, 2 * LEVELS, P], U8)
        mod = put("mod", [P, 48, 2])
        csil = put("c_silu", [P, KD, 2])
        scale1 = put("norm_scale1", [P, KD, 2])
        scale2 = put("norm_scale2", [P, KD, 2])
        lb = put("lower_bound", [P, 8])
        lb1 = put("one_minus_lb", [P, 8])
        dec = put("chunk_decay", [P, 2, HEADS, CH])
        gone = top[0]
        pw = put("powers", [P, BLK + 1, 2, 32])
        pwr = put("powers_reversed", [P, BLK + 1, 2, 32])
        bbar = put("b_bar", [P, 2, 2, PAIRS * GC + GC])
        arep = put("decay_re", [P, SLOT])
        aimp = put("decay_im", [P, SLOT])
        lt = put("lam_tmp", [P, 12, 32])
        sc1 = put("scan_tmp1", [P, 2, SLOT])
        sc2 = put("scan_tmp2", [P, 2, SLOT])
        dmat = put("skip_diag", [P, 8, GC])
        small_end = top[0]
        h_t = put("h_t", [P, KD, TOK])
        ring0 = top[0]
        ring = put("weight_ring", [P, RING, KD, P])
        qs0 = top[0]
        q = put("q", [P, HEADS, TOK])
        ff0 = top[0]
        ff = put("f_fwd", [P, HEADS, TOK])
        fb = put("f_bwd", [P, HEADS, TOK])
        v = put("v", [P, CH, 512])
        pool0 = top[0]
        gt = put("g_lhs", [P, 2, 2, PAIRS, P])
        put("output_matrices_rest", [P, 1024])
        xh0 = top[0]
        xh = put("block_states", [P, NB + 1, SLOT])
        uf0 = top[0]
        uf = put("u_blocks", [P, GROUPS, NB])
        tmp0 = top[0]
        tmp = put("tmp", [P, 2560])
        w0 = top[0]
        wt = put("toeplitz", [P, 4, 8, P])
        end = top[0]
        assert base + end <= nc.sbuf_usable_end, (base + end, nc.sbuf_usable_end)

        x_tt = at("x_t_sb", ff0, [P, KD, TOK])
        x_sq = at("x_squared", uf0, [P, KD, TOK])
        mask_f = at("masks_f32", ff0 + 20480, [P, 2 * LEVELS, P])
        rms = at("rms", qs0, [P, 2, HALF])
        u_perm = at("u_permuted", w0, [P, 4, BLK, NB])
        gpre = [at("g_pre0", xh0, [P, 2, PAIRS, BLK, GC]), at("g_pre1", ff0, [P, 2, PAIRS, BLK, GC])]
        m_lhs = at("m_lhs", pool0, [P, 2, 2, PAIRS, BLK + 1, GC])
        kc = at("kernels", tmp0, [P, 8, KW])
        yg = at("s5_out", tmp0, [P, GROUPS, NB])
        g_t = at("gelu_t", uf0, [P, 4, TOK])
        sig_glu = at("glu_gate", tmp0, [P, 2, HALF])
        ys0 = end - 4 * TOK * 4
        y_s5 = at("y_s5", ys0, [P, 4, TOK])
        kf = at("k_fwd", pool0, [P, HEADS, TOK])
        kb = at("k_bwd", pool0 + 10240, [P, HEADS, TOK])
        ex = at("exp_tmp", pool0 + 20480, [P, HEADS, TOK])
        node_x = [at("node_x0", pool0 + 30720, [P, HEADS, TOK]), at("node_x1", pool0 + 40960, [P, HEADS, TOK])]
        att = at("att", pool0 + 51200, [P, CH, HEADS, P])
        kd_t = at("kd_t", pool0 + 51200, [P, CH, HEADS, P])
        st = at("hg_states", pool0 + 61440, [P, 2, CH, HEADS, P])
        assert pool0 + 61440 + 20480 <= ys0
        g_hg = at("g_out", pool0, [P, HEADS, TOK])
        o_sq = at("o_squared", pool0 + 10240, [P, HEADS, P])
        orms = at("o_rms", pool0 + 12288, [P, HEADS, P])
        o_sb = at("o_sb", pool0 + 14336, [P, 2, HEADS, P])
        y_hg = at("y_hg", pool0 + 20480, [P, HEADS, TOK])
        merged = at("merged", qs0, [P, KD, TOK])
        gates = at("gates", qs0 + 20480, [P, 2, 2, 2, HALF])
        mtmp = at("merge_tmp", qs0 + 30720, [P, 2, HALF])
        diag = at("row_diag", qs0 + 33280, [P, 2, 512])
        a2_row = at("scale2_row", pool0, [P, 2, D])
        b2_row = at("shift2_row", pool0 + 8192, [P, 2, D])
        wo = at("w_out_sb", pool0 + 30720, [P, KD, D])
        xp = at("x_and_pos", pool0 + 63488, [P, 2, 2, D])
        x2 = at("x2", small_end, [P, CH, D])
        g2_row = at("gate2_row", ring0, [P, 2, D])
        nf_row = at("norm_f_row", ring0 + 8192, [P, D])
        g1_row = at("gate1_row", ring0 + 12288, [P, 2, D])
        h2 = at("h2", qs0 + 20480, [P, CH, D])
        h2_t = at("h2_t", qs0, [P, KD, TOK])
        zero = at("zero", pool0 + 32768, [P, D])
        rt = at("router_tiles", gone, [P, 24, CH * EXPERTS])
        rcmp = at("router_compare", gone + 24 * 320, [P, 2, CH * EXPERTS * EPG])
        rint = at("router_ints", gone + 24 * 320 + 2560, [P, 64], I32)
        rms2 = at("row_rms", gone + 24 * 320 + 2560 + 256, [P, 8 * CH])
        rw = at("router_w_sb", gone + 24 * 320 + 2560 + 448, [P, KD, EXPERTS])
        assert gone + 24 * 320 + 2560 + 448 + 512 <= small_end
        w_slot = [at(f"expert_w{s}", end - (s + 1) * 4096, [P, KD, P]) for s in range(3 * KF)]
        x_blk = at("x_block", qs0, [P, D])
        x_blk_t = at("x_block_t", qs0 + 4096, [P, KD, P])
        act_t = at("act_t", qs0 + 8192, [P, KF, P])
        y_blk = at("y_block", qs0 + 12288, [P, D])
        silu = at("silu_tmp", qs0 + 16384, [P, 2, P])
        got = [at(f"gathered{i}", pool0 + i * 4096, [P, D]) for i in range(2 * CH)]
        fin = [at(f"final{i}", pool0 + (10 + i) * 4096, [P, D]) for i in range(CH)]
        fsq = at("final_sq", pool0 + 15 * 4096, [P, D])

        ps = ctx.enter_context(nc.psum_tensor("ps", [P, 8, 512], F32))

        def pair(job):
            n = job % 3
            return ps[:, 2 * n:2 * n + 2, 0:HALF]

        def pair_flat(job):
            n = job % 3
            return ps[:, 2 * n:2 * n + 2, :]

        def bank(job):
            return ps[:, 6 + job % 2, :]

        u_dram = nc.dram_tensor("u_scratch", [4, P, BLK, NB], F32, kind="Internal").ap()
        g_dram = nc.dram_tensor("g_scratch", [GROUPS, GC, BLK, NB], F32, kind="Internal").ap()
        x_sorted = nc.dram_tensor("x_sorted", [(NBLK + 1) * P, D], F32, kind="Internal").ap()
        y_sorted = nc.dram_tensor("y_sorted", [NBLK * P, D], F32, kind="Internal").ap()

        small_in = sem("small_in")
        x_in = sem("x_in")
        const_in = sem("const_in")
        masks_in = sem("masks_in")
        tile_in = [sem(f"tile_in{s}") for s in range(RING)]
        tile_used = sem("tile_used")
        y_hg_ready = sem("y_hg_ready")
        wo_in = sem("wo_in")
        hg_out = sem("hg_out")
        xp_in = [sem(f"xp_in{s}") for s in range(2)]
        norm_f_in = sem("norm_f_in")
        x2_ready = sem("x2_ready")
        h2_ready = sem("h2_ready")
        x_scattered = sem("x_scattered")
        gu_in = [sem(f"gu_in{s}") for s in range(KF)]
        dn_in = [sem(f"dn_in{s}") for s in range(KF)]
        route_ready = sem("route_ready")
        gu_done = sem("gu_done")
        down_done = sem("down_done")
        fin_ready = sem("fin_ready")
        out_done = sem("out_done")
        s5_out = sem("s5_out")
        pool_step = sem("pool_step")
        mask_ready = sem("mask_ready")
        act_took = sem("act_took")
        u_stored = sem("u_stored")
        u_loaded = sem("u_loaded")
        zeroed = sem("zeroed")
        for_act = sem("for_act")
        m_ready = sem("m_ready")
        kc_ready = sem("kc_ready")
        w_loaded = sem("w_loaded")
        w_loaded_act = sem("w_loaded_act")
        scan_done = sem("scan_done")
        g_stored = sem("g_stored")
        g_loaded = sem("g_loaded")
        y_s5_ready = sem("y_s5_ready")
        hg0_in = sem("hg0_in")
        states_ready = sem("states_ready")
        rw_in = sem("rw_in")
        x_blk_in = sem("x_blk_in")
        y_copied = sem("y_copied")
        y_free = sem("y_free")
        xt_done = sem("xt_done")
        y_stored = sem("y_stored")
        blocks_done = sem("blocks_done")
        got_in = [sem(f"got_in{s}") for s in range(CH)]
        c_ready = sem("c_ready")
        step_ready = sem("step_ready")
        lb_sub = sem("lb_sub")
        lb_exp = sem("lb_exp")
        x_ready = sem("x_ready")
        sq_ready = sem("sq_ready")
        angle_ready = sem("angle_ready")
        sin_ready = sem("sin_ready")
        f_pos = sem("f_pos")
        f_log = sem("f_log")
        glu_used = sem("glu_used")
        b_ready = sem("b_ready")
        dec_ready = sem("dec_ready")
        e_sub = sem("e_sub")
        e_exp = sem("e_exp")
        for_dve = sem("for_dve")
        node_ready = sem("node_ready")
        dve_took = sem("dve_took")
        osq_ready = sem("osq_ready")
        ss2_sum = sem("ss2_sum")
        ss2_ready = sem("ss2_ready")
        xt_copied = sem("xt_copied")
        silu_ready = sem("silu_ready")
        x3_ready = sem("x3_ready")
        fss_sum = sem("fss_sum")
        fss_ready = sem("fss_ready")
        dve_step = sem("dve_step")
        gpre_ready = sem("gpre_ready")
        h_ready = sem("h_ready")
        kd_ready = sem("kd_ready")
        diag_ready = sem("diag_ready")
        att_ready = sem("att_ready")
        qd_ready = sem("qd_ready")
        merged_ready = sem("merged_ready")
        row_diag = sem("row_diag")
        sel_ready = sem("sel_ready")
        prod_ready = sem("prod_ready")

        n = 0
        A = {}
        for name, count in (("ss1", 1), ("u", 4), ("q", 4), ("gt", 8), ("x", 8), ("ff", 4), ("fb", 4), ("v", 5),
                            ("y", 4), ("glu", 4), ("kt", 10), ("g", 4), ("oss", 5), ("gate", 16), ("h2t", 5),
                            ("logit", 1)):
            A[name] = n
            n += count
        n = 0
        V = {}
        for name, count in (("ada1", 1), ("k", 4), ("ada2", 1), ("ada_y", 1), ("kv", 8), ("diag", 5), ("node", 14 * (CH + 1)), ("o", 5),
                            ("br", 32), ("row", 16), ("wo", 10), ("prefix", 1)):
            V[name] = n
            n += count

        def par(name):
            a, m = SMALL[name]
            return sm[:, a:a + m]

        def con(name):
            a, m = CONST[name]
            return cst[:, a:a + m]

        def bc(ap, axis, m):
            shape = list(ap.shape)
            return ap.unsqueeze(axis).broadcast_to(tuple(shape[:axis] + [m] + shape[axis:]))

        ident, ones = con("ident"), con("ones")
        START = 36

        STEPS = [(d, l) for d in range(2) for l in range(LEVELS)]
        ADA_AT = [16 + ADA_MID + (32 - ADA_MID) * s // len(STEPS) for s in range(len(STEPS) + 1)]

        block = ctx.enter_context(nc.Block())

        @block.sync
        def _(sp):
            sp.dma_start(sm[:, :], small).then_inc(small_in, 16)
            for s in range(RING):
                sp.dma_start(ring[:, s, :, :], stream[s, :, :, :]).then_inc(tile_in[s], 16)
                if s == 1:
                    sp.dma_start(x_tt[:, :, :], x_t).then_inc(x_in, 16)
                    sp.dma_start(cst[:, :], const).then_inc(const_in, 16)
            sp.dma_start(mask_f[:, :, :], masks).then_inc(masks_in, 16)
            with sp.Fori(1, TILES // RING) as i:
                for s in range(RING):
                    sp.wait_ge(tile_used, i * RING + (s - RING + 1))
                    sp.dma_start(ring[:, s, :, :], stream[bass.ds(i * RING + s, 1), :, :, :]
                                 .rearrange("a p k c -> p (a k) c")).then_inc(tile_in[s], 16)
            for t in range(TILES // RING * RING, TILES):
                sp.wait_ge(tile_used, t - RING + 1)
                sp.dma_start(ring[:, t % RING, :, :], stream[t, :, :, :]).then_inc(tile_in[t % RING], 16)
            sp.wait_ge(y_hg_ready, CH)
            sp.dma_start(wo[:, :, :], w_out).then_inc(wo_in, 16)
            sp.wait_ge(hg_out, 32)
            for c in range(2):
                sp.dma_start(xp[:, c, 0, :], x_rows[c, :, :]).then_inc(xp_in[c], 16)
                sp.dma_start(xp[:, c, 1, :], pos_rows[c, :, :]).then_inc(xp_in[c], 16)
            sp.wait_ge(tile_used, TILES)
            sp.dma_start(nf_row[:, :], norm_f[0:1, :].partition_broadcast(P)).then_inc(norm_f_in, 16)
            for c in range(2, CH):
                sp.wait_ge(x2_ready, c - 1)
                sp.dma_start(xp[:, c % 2, 0, :], x_rows[c, :, :]).then_inc(xp_in[c % 2], 16)
                if c < SCH:
                    sp.dma_start(xp[:, c % 2, 1, :], pos_rows[c, :, :]).then_inc(xp_in[c % 2], 16)
            sp.wait_ge(h2_ready, CH)
            for f in range(KF):
                if f == KF - 1:
                    sp.wait_ge(x_scattered, 16 * 2 * CH)
                sp.dma_start(w_slot[3 * f][:, :, :], w_gate[0, f, :, :, :]).then_inc(gu_in[f], 16)
                sp.dma_start(w_slot[3 * f + 1][:, :, :], w_up[0, f, :, :, :]).then_inc(gu_in[f], 16)
                sp.dma_start(w_slot[3 * f + 2][:, :, :], w_down[0, f, :, :, :]).then_inc(dn_in[f], 16)
            sp.wait_ge(route_ready, 1)
            with sp.Fori(1, EXPERTS) as e:
                b = sp.value_load(rint[0:1, bass.ds(e + START, 1)], min_val=0, max_val=NBLK)
                for f in range(KF):
                    sp.wait_ge(gu_done, b * KF + (f + 1))
                    sp.dma_start(w_slot[3 * f][:, :, :], w_gate[bass.ds(e, 1), f, :, :, :]
                                 .rearrange("a p k c -> p (a k) c")).then_inc(gu_in[f], 16)
                    sp.dma_start(w_slot[3 * f + 1][:, :, :], w_up[bass.ds(e, 1), f, :, :, :]
                                 .rearrange("a p k c -> p (a k) c")).then_inc(gu_in[f], 16)
                    sp.wait_ge(down_done, b * KF + (f + 1))
                    sp.dma_start(w_slot[3 * f + 2][:, :, :], w_down[bass.ds(e, 1), f, :, :, :]
                                 .rearrange("a p k c -> p (a k) c")).then_inc(dn_in[f], 16)
            for c in range(CH):
                sp.wait_ge(fin_ready, c + 1)
                sp.dma_start(y_rows[c, :, :], fin[c][:, :]).then_inc(out_done, 16)
            sp.wait_ge(out_done, 16 * CH)
            sp.wait_ge(s5_out, 16)

        def dest(c, j):
            return rint[:, 26 + 5 * j + c:27 + 5 * j + c]

        def toeplitz(eng, which, loaded):
            for s in which:
                lo = (BLK - 1 - s) * GC
                for r in range(4):
                    eng.dma_start(wt[s * GC:(s + 1) * GC, r, :, :],
                                  kc[r * 32:r * 32 + GC, :, lo:lo + P]).then_inc(loaded, 16)

        @block.gpsimd
        def _(pool):
            steps = [0]

            def done(ins):
                steps[0] += 1
                ins.then_inc(pool_step, 1)
                pool.wait_ge(pool_step, steps[0])

            pool.wait_ge(masks_in, 16)
            nc.gpsimd.tensor_copy(mask[:, :, :], mask_f[:, :, :]).then_inc(mask_ready, 1)
            pool.wait_ge(mask_ready, 1)
            pool.wait_ge(act_took, A["u"] + 4)
            pool.dma_start(u_dram.rearrange("m p s b -> p m (s b)"),
                           u_perm[:, :, :, :].rearrange("p m s b -> p m (s b)")).then_inc(u_stored, 16)
            pool.wait_ge(u_stored, 16)
            u_src = u_dram.rearrange("m p s b -> (m p) s b").rearrange("(g c) s b -> s c g b", c=GC)
            for s in range(BLK):
                pool.dma_start(uf[s * GC:(s + 1) * GC, :, :], u_src[s, :, :, :]).then_inc(u_loaded, 16)
            done(nc.gpsimd.memset(zero[:, :], 0.0))
            for b in range(NBLK + 1):
                pool.dma_start(x_sorted[b * P:(b + 1) * P, :], zero[:, :]).then_inc(zeroed, 16)
            for b in range(EXPERTS, NBLK):
                pool.dma_start(y_sorted[b * P:(b + 1) * P, :], zero[:, :]).then_inc(zeroed, 16)
            pool.wait_ge(zeroed, 16 * (NBLK + 1 + OVER))
            pool.wait_ge(for_act, A["x"] + 8)
            for d in range(2):
                table = pw if d == 0 else pwr
                c_re = bc(par("c_re").rearrange("p (g c) -> p g c", c=GC), 2, BLK + 1)
                c_im = bc(par("c_im").rearrange("p (g c) -> p g c", c=GC), 2, BLK + 1)
                p_re = bc(table[:, :, 0, d * PAIRS:(d + 1) * PAIRS].rearrange("p n g -> p g n"), 3, GC)
                p_im = bc(table[:, :, 1, d * PAIRS:(d + 1) * PAIRS].rearrange("p n g -> p g n"), 3, GC)
                t = tmp[:, 0:PAIRS * (BLK + 1) * GC].rearrange("p (g n c) -> p g n c", g=PAIRS, c=GC)
                m_re, m_im = m_lhs[:, d, 0, :, :, :], m_lhs[:, d, 1, :, :, :]
                done(nc.gpsimd.tensor_tensor(m_re, c_re, p_re, ALU.mult))
                done(nc.gpsimd.tensor_tensor(t, c_im, p_im, ALU.mult))
                done(nc.gpsimd.tensor_tensor(m_re, m_re, t, ALU.subtract))
                done(nc.gpsimd.tensor_tensor(m_im, c_re, p_im, ALU.mult))
                done(nc.gpsimd.tensor_tensor(t, c_im, p_re, ALU.mult))
                done(nc.gpsimd.tensor_tensor(m_im, m_im, t, ALU.add))
                nc.gpsimd.tensor_scalar(m_im, m_im, -1.0, None, ALU.mult).then_inc(m_ready, 1)
            pool.wait_ge(kc_ready, 1)
            toeplitz(pool, (0, 1), w_loaded)
            pool.wait_ge(scan_done, 1)
            pool.dma_start(s5_new, xh[:, NB, :]).then_inc(s5_out, 16)
            pool.wait_ge(act_took, A["y"] + 4)
            g_dst = g_dram.rearrange("g c t b -> t c g b")
            for t8 in range(BLK):
                pool.dma_start(g_dst[t8, :, :, :], yg[t8 * GC:(t8 + 1) * GC, :, :]).then_inc(g_stored, 16)
            pool.wait_ge(g_stored, 16 * BLK)
            pool.dma_start(g_t[:, :, :], g_dram.rearrange("g c t b -> (g c) (t b)")
                           .rearrange("(m p) n -> p m n", p=P)).then_inc(g_loaded, 16)
            pool.wait_ge(y_s5_ready, 1)
            pool.dma_start(st[:, 0, 0, :, :], hg_state[0, :, :, :].rearrange("h d v -> d h v")).then_inc(hg0_in, 16)
            pool.dma_start(st[:, 1, SCH - 1, :, :], hg_state[1, :, :, :].rearrange("h d v -> d h v"))\
                .then_inc(hg0_in, 16)
            pool.wait_ge(states_ready, 1)
            for d in range(2):
                pool.dma_start(hg_new[d, :, :, :].rearrange("h d v -> d h v"), st[:, d, SCH, :, :])\
                    .then_inc(hg_out, 16)
            pool.dma_start(rw[:, :, :], router_w).then_inc(rw_in, 16)
            pool.wait_ge(route_ready, 1)
            pool.wait_ge(h2_ready, CH)
            for c in range(CH):
                for j in range(2):
                    pool.indirect_dma_start(out=x_sorted, out_offset=bass.IndirectOffsetOnAxis(ap=dest(c, j), axis=0),
                                            in_=h2[:, c, :], in_offset=None).then_inc(x_scattered, 16)
            pool.wait_ge(x_scattered, 16 * 2 * CH)
            pool.dma_start(x_blk[:, :], x_sorted[0:P, :]).then_inc(x_blk_in, 16)
            pool.sem_inc(y_copied, 1)
            pool.sem_inc(y_free, 1)
            blocks = pool.value_load(rint[0:1, 25:26], min_val=EXPERTS, max_val=NBLK)
            with pool.Fori(0, NBLK) as i:
                with pool.If(i < blocks):
                    pool.wait_ge(xt_done, i + 1)
                    pool.dma_start(x_blk[:, :], x_sorted[bass.ds(i * P + P, P), :]).then_inc(x_blk_in, 16)
                    pool.wait_ge(y_copied, i * 2 + 3)
                    pool.dma_start(y_sorted[bass.ds(i * P, P), :], y_blk[:, :]).then_inc(y_stored, 16)
                    pool.wait_ge(y_stored, i * 16 + 16)
                    pool.sem_inc(y_free, 1)
                pool.nop()
            pool.wait_ge(x_blk_in, blocks * 16 + 16)
            pool.sem_inc(blocks_done, 1)
            pool.wait_ge(blocks_done, 1)
            for c in range(CH):
                for j in range(2):
                    pool.indirect_dma_start(out=got[2 * c + j][:, :], out_offset=None, in_=y_sorted,
                                            in_offset=bass.IndirectOffsetOnAxis(ap=dest(c, j), axis=0))\
                        .then_inc(got_in[c], 16)

        @block.scalar
        def _(act):
            eps = con("eps")

            act.wait_ge(small_in, 16)
            nc.scalar.activation(csil[:, :, :], par("cvec").rearrange("p (k v) -> p k v", v=2), ACT.Silu)\
                .then_inc(c_ready, 1)
            nc.scalar.activation(lt[:, 2, :], par("log_step"), ACT.Exp).then_inc(step_ready, 1)
            act.wait_ge(lb_sub, 1)
            nc.scalar.activation(lb[:, :], lb[:, :], ACT.Exp).then_inc(lb_exp, 1)
            act.wait_ge(x_ready, 1)
            nc.scalar.activation(x_sq[:, :, :], x_tt[:, :, :], ACT.Square).then_inc(sq_ready, 1)
            act.wait_ge(angle_ready, 1)
            nc.scalar.activation(lt[:, 3, :], lt[:, 8, :], ACT.Exp)
            nc.scalar.activation(lt[:, 6, :], lt[:, 4, :], ACT.Sin)
            nc.scalar.activation(lt[:, 7, :], lt[:, 4, :], ACT.Sin, scale=0.5).then_inc(sin_ready, 1)
            act.wait_ge(const_in, 16)
            act.wait_ge(for_act, A["ss1"] + 1)
            nc.scalar.activation(rms[:, :, :], pair(A["ss1"]), ACT.Sqrt, scale=1.0 / D, bias=eps)\
                .then_inc(act_took, 1)

            def take(job, out, func, src=None, **kw):
                act.wait_ge(for_act, job + 1)
                nc.scalar.activation(out, pair(job) if src is None else src, func, **kw).then_inc(act_took, 1)

            def halves(ap):
                return ap.rearrange("p (a t) -> p a t", a=2)

            for m in range(4):
                act.wait_ge(for_act, A["u"] + m + 1)
                for a in range(2):
                    last = nc.scalar.activation(u_perm[:, m, :, a * (NB // 2):(a + 1) * (NB // 2)],
                                                pair(A["u"] + m)[:, a, :].rearrange("p (b s) -> p s b", s=BLK), ACT.Copy)
                last.then_inc(act_took, 1)
            for m in range(4):
                take(A["q"] + m, halves(q[:, m, :]), ACT.Silu)
            for n in range(8):
                d, ri, half = n // 4, n // 2 % 2, n % 2
                job = A["gt"] + n
                take(job, gt[:, d, ri, 8 * half:8 * half + 8, :].rearrange("p (a i) c -> p a (i c)", a=2), ACT.Copy,
                     pair_flat(job))
            for n in range(8):
                d, ri, half = n // 4, n // 2 % 2, n % 2
                job = A["x"] + n
                c0 = d * 32 + ri * PAIRS + 8 * half
                src = pair(job).rearrange("p a (i b) -> p a i b", b=NB)
                act.wait_ge(for_act, job + 1)
                one = src[:, :, :, 0:SB - 1] if d == 0 else src[:, :, :, SB - 1:0:-1]
                two = src[:, :, :, SB:NB] if d == 0 else src[:, :, :, NB - 1:SB - 1:-1]
                nc.scalar.activation(xh[:, 1:SB, c0:c0 + 8].rearrange("p s (a i) -> p a i s", a=2), one, ACT.Copy)
                nc.scalar.activation(xh[:, SB + 1:NB + 1, c0:c0 + 8].rearrange("p s (a i) -> p a i s", a=2), two,
                                     ACT.Copy).then_inc(act_took, 1)
            for m in range(4):
                take(A["ff"] + m, halves(ff[:, m, :]), ACT.Sigmoid)
            for m in range(4):
                take(A["fb"] + m, halves(fb[:, m, :]), ACT.Sigmoid)
            act.wait_ge(mask_ready, 1)
            for c in range(CH):
                take(A["v"] + c, v[:, c, :], ACT.Copy, pair_flat(A["v"] + c)[:, 0, :])
            act.wait_ge(kc_ready, 1)
            toeplitz(act, range(2, BLK), w_loaded_act)
            act.wait_ge(w_loaded_act, 16 * 24)
            act.wait_ge(w_loaded, 16 * 8)
            for n in range(4):
                take(A["y"] + n, yg[:, 8 * n:8 * n + 8, :].rearrange("p (i a) b -> p a i b", a=2),
                     ACT.Gelu_apprx_tanh, pair(A["y"] + n).rearrange("p a (i b) -> p a i b", b=NB))
            for d in range(2):
                f_all = ff if d == 0 else fb
                act.wait_ge(f_pos, d + 1)
                nc.scalar.activation(f_all[:, :, :], f_all[:, :, :], ACT.Ln)
                nc.scalar.activation(ex[:, :, :], ex[:, :, :], ACT.Ln).then_inc(f_log, 1)
            act.wait_ge(g_loaded, 16)
            for m in range(4):
                if m >= 1:
                    act.wait_ge(glu_used, m)
                take(A["glu"] + m, sig_glu[:, :, :], ACT.Sigmoid, bias=par("b_glu")[:, m:m + 1])
            act.wait_ge(b_ready, 2)
            for d in range(2):
                f_all = ff if d == 0 else fb
                at_end = f_all[:, :, :].rearrange("p h (c t) -> p h c t", t=P)[:, :, :, P - 1 if d == 0 else 0]
                last = nc.scalar.activation(dec[:, d, :, :], at_end, ACT.Exp)
            last.then_inc(dec_ready, 1)

            def exp_in_place(n):
                act.wait_ge(e_sub, n)
                nc.scalar.activation(ex[:, :, :], ex[:, :, :], ACT.Exp).then_inc(e_exp, 1)

            exp_in_place(1)
            exp_in_place(2)
            act.wait_ge(y_s5_ready, 1)
            for n in range(10):
                d, c = divmod(n, CH)
                if n == CH:
                    act.wait_ge(for_dve, V["kv"] + 4)
                job = A["kt"] + n
                take(job, kd_t[:, c, :, :].rearrange("p h d -> p (h d)"), ACT.Copy, pair_flat(job)[:, 0, :])
            for n in range(len(STEPS)):
                exp_in_place(3 + n)
            for d in range(2):
                act.wait_ge(e_sub, 17 + d)
                nc.scalar.activation(ex[:, :, :], (ff if d == 0 else fb)[:, :, :], ACT.Exp).then_inc(e_exp, 1)
            act.wait_ge(node_ready, len(STEPS))
            for m in range(4):
                take(A["g"] + m, halves(g_hg[:, m, :]), ACT.Silu)
            for c in range(CH):
                act.wait_ge(dve_took, V["o"] + c + 1)
                nc.scalar.activation(o_sq[:, :, :], o_sb[:, c % 2, :, :], ACT.Square).then_inc(osq_ready, 1)
                if c >= 1:
                    act.wait_ge(y_hg_ready, c)
                job = A["oss"] + c
                take(job, orms[:, :, :].rearrange("p h t -> p (h t)"), ACT.Sqrt, pair_flat(job)[:, 0, :],
                     scale=1.0 / P, bias=eps)
            for m in range(KD):
                for w in range(2):
                    if m >= 2:
                        act.wait_ge(dve_took, V["br"] + 4 * (m - 2) + 2 * w + 2)
                    take(A["gate"] + 2 * m + w, gates[:, m % 2, w, :, :], ACT.Sigmoid)
            for c in range(CH):
                act.wait_ge(x2_ready, c + 1)
                nc.scalar.activation(h2[:, c, :], x2[:, c, :], ACT.Square, accum_out=rms2[:, c:c + 1])\
                    .then_inc(ss2_sum, 1)
                act.wait_ge(ss2_sum, c + 1)
                nc.scalar.activation(rms2[:, 8 + c:9 + c], rms2[:, c:c + 1], ACT.Sqrt, scale=1.0 / D, bias=eps)\
                    .then_inc(ss2_ready, 1)
            for c in range(CH):
                job = A["h2t"] + c
                act.wait_ge(for_act, job + 1)
                nc.scalar.activation(h2_t[:, :, c * P:(c + 1) * P].rearrange("p (a k) t -> p a k t", a=2),
                                     pair_flat(job).rearrange("p a (k t) -> p a k t", t=P), ACT.Copy)\
                    .then_inc(act_took, 1)
            take(A["logit"], rt[:, 0, :], ACT.Sigmoid, pair_flat(A["logit"])[:, 0, 0:CH * EXPERTS])
            act.wait_ge(route_ready, 1)
            blocks = act.value_load(rint[0:1, 25:26], min_val=EXPERTS, max_val=NBLK)

            def copy_x():
                for a in range(2):
                    last = nc.scalar.activation(x_blk_t[:, 4 * a:4 * a + 4, :].rearrange("p k t -> p (k t)"),
                                                ps[:, 6 + a, :], ACT.Copy)
                last.then_inc(xt_copied, 1)

            act.wait_ge(xt_done, 1)
            copy_x()
            with act.Fori(0, NBLK) as i:
                with act.If(i < blocks):
                    for f in range(KF):
                        act.wait_ge(gu_done, i * KF + f + 1)
                        nc.scalar.activation(silu[:, f % 2, :], ps[:, f % 2, 0:P], ACT.Silu).then_inc(silu_ready, 1)
                    act.wait_ge(xt_done, i + 2)
                    copy_x()
                    act.wait_ge(down_done, i * KF + KF)
                    act.wait_ge(y_free, i + 1)
                    nc.scalar.activation(y_blk[:, 0:512], ps[:, 4, :], ACT.Copy).then_inc(y_copied, 1)
                act.nop()
            for c in range(CH):
                act.wait_ge(x3_ready, c + 1)
                nc.scalar.activation(fsq[:, :], fin[c][:, :], ACT.Square, accum_out=rms2[:, 16 + c:17 + c])\
                    .then_inc(fss_sum, 1)
                act.wait_ge(fss_sum, c + 1)
                nc.scalar.activation(rms2[:, 24 + c:25 + c], rms2[:, 16 + c:17 + c], ACT.Sqrt, scale=1.0 / D, bias=eps)\
                    .then_inc(fss_ready, 1)

        @block.vector
        def _(dve):
            steps = [0]
            vec = nc.vector

            def note(ins):
                steps[0] += 1
                ins.then_inc(dve_step, 1)

            def settle():
                dve.wait_ge(dve_step, steps[0])

            def done(ins):
                note(ins)
                settle()

            def took(ins, job):
                ins.then_inc(dve_took, 1)
                dve.wait_ge(dve_took, job + 1)

            def pos_add():
                xs = x_tt[:, :, 0:SAMPLE].rearrange("p k (r c) -> p k r c", c=64)
                row = bc(par("pos_row").rearrange("p (k r) -> p k r", r=8), 3, 64)
                col = bc(par("pos_col").rearrange("p (k c) -> p k c", c=64), 2, 8)
                for k in range(4):
                    vec.tensor_tensor(xs[:, k, :, :], xs[:, k, :, :], row[:, k, :, :], ALU.add)
                    last = vec.tensor_tensor(xs[:, 4 + k, :, :], xs[:, 4 + k, :, :], col[:, k, :, :], ALU.add)
                last.then_inc(x_ready, 1)

            def norm2(c):
                cv = 0 if c < SCH else 1
                dve.wait_ge(ss2_ready, c + 1)
                done(vec.reciprocal(rms2[:, 8 + c:9 + c], rms2[:, 8 + c:9 + c]))
                done(vec.scalar_tensor_tensor(h2[:, c, :], x2[:, c, :], rms2[:, 8 + c:9 + c], a2_row[:, cv, :],
                                                    ALU.mult, ALU.mult))
                vec.tensor_tensor(h2[:, c, :], h2[:, c, :], b2_row[:, cv, :], ALU.add).then_inc(h2_ready, 1)

            def final(c):
                dve.wait_ge(fss_ready, c + 1)
                if c == 0:
                    dve.wait_ge(norm_f_in, 16)
                done(vec.reciprocal(rms2[:, 24 + c:25 + c], rms2[:, 24 + c:25 + c]))
                vec.scalar_tensor_tensor(fin[c][:, :], fin[c][:, :], rms2[:, 24 + c:25 + c], nf_row[:, :], ALU.mult,
                                               ALU.mult).then_inc(fin_ready, 1)

            dve.wait_ge(small_in, 16)
            vec.tensor_tensor(lb[:, :], par("lb_logits"), par("lb_logits"), ALU.subtract).then_inc(lb_sub, 1)
            dve.wait_ge(x_in, 16)
            pos_add()
            lr, step, mag, ang, kk, sn, sh, tt, den, fr, fi = (lt[:, j, :] for j in (0, 2, 3, 4, 5, 6, 7, 8, 9, 10, 11))
            li = par("lam_im")
            done(vec.tensor_scalar(lr, par("lam_re"), -1e-4, None, ALU.min))
            dve.wait_ge(step_ready, 1)
            note(vec.tensor_tensor(tt, lr, step, ALU.mult))
            done(vec.tensor_tensor(ang, li, step, ALU.mult))
            done(vec.tensor_scalar(kk, ang, 1.0 / TWO_PI, MAGIC, ALU.mult, ALU.add))
            done(vec.tensor_scalar(kk, kk, MAGIC, None, ALU.subtract))
            for part in (6.28125, 0.0019340515136718750, 1.2556659146e-06):
                done(vec.scalar_tensor_tensor(ang, kk, -part, ang, ALU.mult, ALU.add))
            vec.tensor_scalar(ang, ang, 3.1415925, -3.1415925, ALU.min, ALU.max).then_inc(angle_ready, 1)
            dve.wait_ge(lb_exp, 1)
            done(vec.reciprocal(lb1[:, :], lb[:, :]))
            done(vec.tensor_tensor(lb[:, :], lb[:, :], lb1[:, :], ALU.mult))
            done(vec.tensor_tensor(lb[:, :], lb[:, :], lb[:, :], ALU.subtract))
            note(vec.tensor_scalar(lb1[:, :], lb[:, :], -1.0, 1.0, ALU.mult, ALU.add))
            note(vec.memset(pw[:, 0, 0, :], 1.0))
            note(vec.memset(pw[:, 0, 1, :], 0.0))
            note(vec.memset(bbar[:, :, :, PAIRS * GC:], 0.0))
            dve.wait_ge(sin_ready, 1)
            done(vec.tensor_tensor(tt, sh, sh, ALU.mult))
            done(vec.tensor_scalar(tt, tt, -2.0, 1.0, ALU.mult, ALU.add))
            note(vec.tensor_tensor(pw[:, 1, 0, :], mag, tt, ALU.mult))
            done(vec.tensor_tensor(pw[:, 1, 1, :], mag, sn, ALU.mult))
            for n in range(1, BLK):
                note(vec.tensor_tensor(pw[:, n + 1, 0, :], pw[:, n, 0, :], pw[:, 1, 0, :], ALU.mult))
                note(vec.tensor_tensor(pw[:, n + 1, 1, :], pw[:, n, 0, :], pw[:, 1, 1, :], ALU.mult))
                note(vec.tensor_tensor(tt, pw[:, n, 1, :], pw[:, 1, 1, :], ALU.mult))
                done(vec.tensor_tensor(kk, pw[:, n, 1, :], pw[:, 1, 0, :], ALU.mult))
                note(vec.tensor_tensor(pw[:, n + 1, 0, :], pw[:, n + 1, 0, :], tt, ALU.subtract))
                done(vec.tensor_tensor(pw[:, n + 1, 1, :], pw[:, n + 1, 1, :], kk, ALU.add))
            note(vec.tensor_copy(pwr[:, :, :, :], pw[:, ::-1, :, :]))
            for ri in range(2):
                lam8 = pw[:, BLK, :, :]
                note(vec.tensor_copy(arep[:, :].rearrange("p (d r g) -> p d r g", d=2, r=2)[:, :, ri, :],
                                     lam8[:, 0, :].rearrange("p (d g) -> p d g", d=2)))
                note(vec.tensor_scalar(aimp[:, :].rearrange("p (d r g) -> p d r g", d=2, r=2)[:, :, ri, :],
                                       lam8[:, 1, :].rearrange("p (d g) -> p d g", d=2), 1.0 if ri else -1.0, None,
                                       ALU.mult))
            nr = mag
            note(vec.tensor_scalar(nr, pw[:, 1, 0, :], -1.0, None, ALU.add))
            note(vec.tensor_tensor(den, lr, lr, ALU.mult))
            done(vec.tensor_tensor(tt, li, li, ALU.mult))
            done(vec.tensor_tensor(den, den, tt, ALU.add))
            note(vec.reciprocal(den, den))
            done(vec.tensor_tensor(fr, nr, lr, ALU.mult))
            done(vec.tensor_tensor(tt, pw[:, 1, 1, :], li, ALU.mult))
            note(vec.tensor_tensor(fr, fr, tt, ALU.add))
            done(vec.tensor_tensor(fi, pw[:, 1, 1, :], lr, ALU.mult))
            done(vec.tensor_tensor(tt, nr, li, ALU.mult))
            done(vec.tensor_tensor(fi, fi, tt, ALU.subtract))
            note(vec.tensor_tensor(fr, fr, den, ALU.mult))
            done(vec.tensor_tensor(fi, fi, den, ALU.mult))
            dve.wait_ge(for_act, A["ss1"] + 1)
            b_re = par("b_re").rearrange("p (g c) -> p g c", c=GC)
            b_im = par("b_im").rearrange("p (g c) -> p g c", c=GC)
            t256 = tmp[:, 0:PAIRS * GC].rearrange("p (g c) -> p g c", c=GC)
            for d in range(2):
                f_re = bc(fr[:, d * PAIRS:(d + 1) * PAIRS], 2, GC)
                f_im = bc(fi[:, d * PAIRS:(d + 1) * PAIRS], 2, GC)
                o_re = bbar[:, 0, d, 0:PAIRS * GC].rearrange("p (g c) -> p g c", c=GC)
                o_im = bbar[:, 1, d, 0:PAIRS * GC].rearrange("p (g c) -> p g c", c=GC)
                note(vec.tensor_tensor(o_re, f_re, b_re, ALU.mult))
                done(vec.tensor_tensor(t256, f_im, b_im, ALU.mult))
                done(vec.tensor_tensor(o_re, o_re, t256, ALU.subtract))
                note(vec.tensor_tensor(o_im, f_re, b_im, ALU.mult))
                done(vec.tensor_tensor(t256, f_im, b_re, ALU.mult))
                done(vec.tensor_tensor(o_im, o_im, t256, ALU.add))

            def input_matrices(d):
                table = pwr[:, 1:BLK + 1, :, :] if d == 0 else pw[:, 0:BLK, :, :]
                p_re = bc(table[:, :, 0, d * PAIRS:(d + 1) * PAIRS].rearrange("p n g -> p g n"), 3, GC)
                p_im = bc(table[:, :, 1, d * PAIRS:(d + 1) * PAIRS].rearrange("p n g -> p g n"), 3, GC)
                bb_re = bc(bbar[:, 0, d, 0:PAIRS * GC].rearrange("p (g c) -> p g c", c=GC), 2, BLK)
                bb_im = bc(bbar[:, 1, d, 0:PAIRS * GC].rearrange("p (g c) -> p g c", c=GC), 2, BLK)
                t = tmp[:, 0:PAIRS * BLK * GC].rearrange("p (g n c) -> p g n c", g=PAIRS, c=GC)
                g_re, g_im = gpre[d][:, 0, :, :, :], gpre[d][:, 1, :, :, :]
                note(vec.tensor_tensor(g_re, p_re, bb_re, ALU.mult))
                done(vec.tensor_tensor(t, p_im, bb_im, ALU.mult))
                done(vec.tensor_tensor(g_re, g_re, t, ALU.subtract))
                note(vec.tensor_tensor(g_im, p_re, bb_im, ALU.mult))
                done(vec.tensor_tensor(t, p_im, bb_re, ALU.mult))
                vec.tensor_tensor(g_im, g_im, t, ALU.add).then_inc(gpre_ready, 1)

            dve.wait_ge(act_took, A["ss1"] + 1)
            done(vec.reciprocal(rms[:, :, :], rms[:, :, :]))
            rstd = rms[:, :, :].rearrange("p a t -> p (a t)")
            note(vec.tensor_tensor(x_tt[:, :, :], x_tt[:, :, :], bc(rstd, 1, KD), ALU.mult))

            def vectors(job, j0, count):
                dve.wait_ge(for_dve, job + 1)
                bias = bc(par("b_ada")[:, j0:j0 + count], 2, 2)
                src = bank(job)[:, 0:2 * count].rearrange("p (j v) -> p j v", v=2)
                took(vec.tensor_tensor(mod[:, j0:j0 + count, :], src, bias, ALU.add), job)

            vectors(V["ada1"], 0, 16)
            done(vec.scalar_tensor_tensor(scale1[:, :, :], mod[:, 8:16, :], 1.0, bc(par("norm1"), 2, 2), ALU.add,
                                          ALU.mult))
            for k in range(KD):
                for cv, (lo, hi) in enumerate(((0, SAMPLE), (SAMPLE, TOK))):
                    last = vec.tensor_scalar(h_t[:, k, lo:hi], x_tt[:, k, lo:hi], scale1[:, k, cv:cv + 1],
                                             mod[:, k, cv:cv + 1], ALU.mult, ALU.add)
            last.then_inc(h_ready, 1)
            dve.wait_ge(h_ready, 1)
            input_matrices(0)
            dve.wait_ge(gpre_ready, 1)
            input_matrices(1)
            done(vec.tensor_tensor(dmat[:, :, :], bc(par("s5_d"), 2, GC), bc(par("id16"), 1, 8), ALU.mult))
            dve.wait_ge(act_took, A["q"] + 4)
            note(vec.tensor_scalar(q[:, :, :], q[:, :, :], float(P) ** -0.5, None, ALU.mult))
            dve.wait_ge(for_act, A["gt"] + 8)
            note(vec.tensor_copy(xh[:, 0, :], par("h0")))
            done(vec.memset(xh[:, SB, :], 0.0))
            dve.wait_ge(act_took, A["x"] + 8)
            for i in range(SB - 1):
                two = i < PB
                h_in = xh[:, i:i + SB + 1:SB, :] if two else xh[:, i:i + 1, :]
                h_out = xh[:, i + 1:i + SB + 2:SB, :] if two else xh[:, i + 1:i + 2, :]
                m = 2 if two else 1
                t1, t2 = sc1[:, 0:m, :], sc2[:, 0:m, :]
                note(vec.tensor_tensor(t1, h_in, bc(arep[:, :], 1, m), ALU.mult))
                for a in range(m):
                    swapped = h_in[:, a, :].rearrange("p (d r g) -> p d r g", d=2, r=2)[:, :, ::-1, :]
                    note(vec.tensor_tensor(t2[:, a, :].rearrange("p (d r g) -> p d r g", d=2, r=2), swapped,
                                           aimp[:, :].rearrange("p (d r g) -> p d r g", d=2, r=2), ALU.mult))
                dve.wait_ge(dve_step, steps[0] - m)
                note(vec.tensor_tensor(t1, t1, h_out, ALU.add))
                settle()
                done(vec.tensor_tensor(h_out, t1, t2, ALU.add))
            vec.nop().then_inc(scan_done, 1)
            for n in range(4):
                job = V["k"] + n
                dve.wait_ge(for_dve, job + 1)
                src = bank(job).rearrange("p (j d c) -> p j d c", j=2, d=2)
                cols = kc[:, 4 * (n // 2) + n % 2:4 * (n // 2) + n % 2 + 3:2, :]
                note(vec.tensor_copy(cols[:, :, 0:P], src[:, :, 1, :]))
                note(vec.tensor_copy(cols[:, :, P:KW], src[:, :, 0, GC:P]))
                settle()
                mid = cols[:, :, P - GC:P]
                took(vec.tensor_tensor(mid, mid, src[:, :, 0, 0:GC], ALU.add), job)
            vec.tensor_tensor(kc[:, :, P - GC:P], kc[:, :, P - GC:P], dmat[:, :, :], ALU.add).then_inc(kc_ready, 1)
            dve.wait_ge(act_took, A["fb"] + 4)
            for d in range(2):
                f_all = ff if d == 0 else fb
                for h in range(HEADS):
                    j = d * HEADS + h
                    note(vec.tensor_scalar(f_all[:, h, :], f_all[:, h, :], lb1[:, j:j + 1], lb[:, j:j + 1], ALU.mult,
                                           ALU.add))
            settle()
            vectors(V["ada2"], 16, ADA_MID - ADA_Y)
            dve.wait_ge(for_act, A["y"] + 4)
            dve.wait_ge(const_in, 16)
            for d in range(2):
                f_all, k_all = (ff, kf) if d == 0 else (fb, kb)
                note(vec.tensor_scalar(k_all[:, :, :], f_all[:, :, :], -1.0, 1.0, ALU.mult, ALU.add))
                done(vec.tensor_scalar(ex[:, :, :], f_all[:, :, :], TINY, 1.0 / TINY, ALU.min, ALU.mult))
                vec.tensor_scalar(f_all[:, :, :], f_all[:, :, :], TINY, None, ALU.max).then_inc(f_pos, 1)
                dve.wait_ge(f_log, d + 1)
                done(vec.tensor_tensor(f_all[:, :, :], f_all[:, :, :], ex[:, :, :], ALU.add))
                for h in range(HEADS):
                    run = f_all[:, h, :] if d == 0 else f_all[:, h, ::-1]
                    keep = con("reset_f") if d == 0 else con("reset_b")[:, ::-1]
                    last = vec.tensor_tensor_scan(run, keep, run, 0.0, ALU.mult, ALU.add)
                last.then_inc(b_ready, 1)
            vectors(V["ada_y"], 16 + ADA_MID - ADA_Y, ADA_Y)
            for m in range(4):
                dve.wait_ge(act_took, A["glu"] + m + 1)
                out = y_s5[:, m, :].rearrange("p (b t) -> p t b", t=BLK)
                src = g_t[:, m, :].rearrange("p (t b) -> p t b", t=BLK)
                gate = sig_glu[:, :, :].rearrange("p a n -> p (a n)").rearrange("p (t b) -> p t b", t=BLK)
                vec.tensor_tensor(out, src, gate, ALU.mult).then_inc(glu_used, 1)
            dve.wait_ge(glu_used, 4)
            vec.nop().then_inc(y_s5_ready, 1)
            dve.wait_ge(s5_out, 16)
            dve.wait_ge(b_ready, 2)
            for d in range(2):
                f_all, k_all = (ff, kf) if d == 0 else (fb, kb)
                b = f_all[:, :, :].rearrange("p h (c t) -> p (h c) t", t=P)
                far = b[:, :, P - 1:P] if d == 0 else b[:, :, 0:1]
                vec.tensor_tensor(ex[:, :, :].rearrange("p h (c t) -> p (h c) t", t=P),
                                  far.broadcast_to((P, HEADS * CH, P)), b, ALU.subtract).then_inc(e_sub, 1)
                dve.wait_ge(e_exp, d + 1)
                vec.tensor_tensor(node_x[d][:, :, :], k_all[:, :, :], ex[:, :, :], ALU.mult).then_inc(kd_ready, 1)
                dve.wait_ge(kd_ready, d + 1)
            dve.wait_ge(hg0_in, 32)
            dve.wait_ge(dec_ready, 1)
            for n in range(8):
                d, c = divmod(n, 4)
                c = (0, 1, 2, SCH)[c] if d == 0 else (3, 2, 1, SCH)[c]
                job = V["kv"] + n
                dve.wait_ge(for_dve, job + 1)
                src = bank(job).rearrange("p (h v) -> p h v", h=HEADS)
                if c == SCH:
                    last = vec.tensor_copy(st[:, d, SCH, :, :], src)
                else:
                    to = c + 1 if d == 0 else c - 1
                    for h in range(HEADS):
                        last = vec.scalar_tensor_tensor(st[:, d, to, h, :], st[:, d, c, h, :], dec[:, d, h, c:c + 1],
                                                        src[:, h, :], ALU.mult, ALU.add)
                took(last, job)
            vec.nop().then_inc(states_ready, 1)
            dve.wait_ge(for_act, A["kt"] + 10)
            vec.tensor_tensor(node_x[1][:, :, :], kf[:, :, :], kb[:, :, :], ALU.add).then_inc(diag_ready, 1)

            def take_diag():
                for c in range(CH):
                    job = V["diag"] + c
                    dve.wait_ge(for_dve, job + 1)
                    took(vec.tensor_tensor(att[:, c, :, :], bank(job).rearrange("p (h t) -> p h t", h=HEADS),
                                           bc(ident, 1, HEADS), ALU.mult), job)

            def take_nodes(s):
                d, l = STEPS[s]
                dve.wait_ge(mask_ready, 1)
                half = (P // 2) >> l
                side = 1 - d

                def queries(ap):
                    return ap.rearrange("p (h n w c) -> p h n w c", h=HEADS, w=2, c=half)[:, :, :, side, :]

                for c in range(CH):
                    job = V["node"] + s * (CH + 1) + c
                    dve.wait_ge(for_dve, job + 1)
                    of = mask[:, d * LEVELS + l, :].rearrange("p (n w c) -> p n w c", w=2, c=half)[:, :, side, :]
                    vec.copy_predicated(queries(att[:, c, :, :].rearrange("p h t -> p (h t)")), bc(of, 1, HEADS),
                                        queries(bank(job))).then_inc(dve_took, 1)

            def take_vectors(s):
                vectors(V["node"] + s * (CH + 1) + CH, ADA_AT[s], ADA_AT[s + 1] - ADA_AT[s])

            for s, (d, l) in enumerate(STEPS):
                half = (P // 2) >> l
                f_all, k_all = (ff, kf) if d == 0 else (fb, kb)

                def nodes(t):
                    return t[:, :, :].rearrange("p h t -> p (h t)").rearrange("p (n w c) -> p n w c", w=2, c=half)

                b, e, x, kv, qv = nodes(f_all), nodes(ex), nodes(node_x[s % 2]), nodes(k_all), nodes(q)
                n = HEADS * TOK // (2 * half)
                left, right = b[:, :, 0, :], b[:, :, 1, :]
                mid = (left[:, :, half - 1:half] if d == 0 else right[:, :, 0:1]).broadcast_to((P, n, half))
                one = vec.tensor_tensor(e[:, :, 0, :], mid, left, ALU.subtract) if d == 0 else \
                    vec.tensor_tensor(e[:, :, 0, :], left, mid, ALU.subtract)
                note(one)
                two = vec.tensor_tensor(e[:, :, 1, :], right, mid, ALU.subtract) if d == 0 else \
                    vec.tensor_tensor(e[:, :, 1, :], mid, right, ALU.subtract)
                two.then_inc(e_sub, 1)
                if s == 0:
                    take_diag()
                else:
                    take_nodes(s - 1)
                dve.wait_ge(e_exp, 3 + s)
                note(vec.tensor_tensor(x[:, :, 0, :], (kv if d == 0 else qv)[:, :, 0, :], e[:, :, 0, :], ALU.mult))
                vec.tensor_tensor(x[:, :, 1, :], (qv if d == 0 else kv)[:, :, 1, :], e[:, :, 1, :], ALU.mult)\
                    .then_inc(node_ready, 1)
                dve.wait_ge(node_ready, s + 1)
                if s > 0:
                    take_vectors(s - 1)
            vec.nop().then_inc(e_sub, 1)
            take_nodes(len(STEPS) - 1)
            take_vectors(len(STEPS) - 1)
            dve.wait_ge(dve_took, V["node"] + (CH + 1) * len(STEPS))
            note(vec.scalar_tensor_tensor(scale2[:, :, :], mod[:, 32:40, :], 1.0, bc(par("norm2"), 2, 2), ALU.add,
                                          ALU.mult))
            vec.nop().then_inc(att_ready, 1)
            for d in range(2):
                dve.wait_ge(e_exp, 17 + d)
                vec.tensor_tensor(node_x[d][:, :, :], q[:, :, :], ex[:, :, :], ALU.mult).then_inc(qd_ready, 1)
                dve.wait_ge(qd_ready, d + 1)
                if d == 0:
                    vec.nop().then_inc(e_sub, 1)
            dve.wait_ge(act_took, A["g"] + 4)

            def finish(c):
                dve.wait_ge(act_took, A["oss"] + c + 1)
                done(vec.reciprocal(orms[:, :, :], orms[:, :, :]))
                done(vec.tensor_tensor(o_sb[:, c % 2, :, :], o_sb[:, c % 2, :, :], orms[:, :, :], ALU.mult))
                for h in range(HEADS):
                    last = vec.scalar_tensor_tensor(y_hg[:, h, c * P:(c + 1) * P], o_sb[:, c % 2, h, :],
                                                    par("hg_norm")[:, h:h + 1], g_hg[:, h, c * P:(c + 1) * P],
                                                    ALU.mult, ALU.mult)
                last.then_inc(y_hg_ready, 1)
                dve.wait_ge(y_hg_ready, c + 1)

            for c in range(CH):
                job = V["o"] + c
                dve.wait_ge(for_dve, job + 1)
                took(vec.tensor_copy(o_sb[:, c % 2, :, :], bank(job).rearrange("p (h t) -> p h t", h=HEADS)), job)
                if c >= 1:
                    finish(c - 1)
            finish(CH - 1)
            for m in range(KD):
                for w in range(2):
                    dve.wait_ge(act_took, A["gate"] + 2 * m + w + 1)
                    for a in range(2):
                        job = V["br"] + 4 * m + 2 * w + a
                        dve.wait_ge(for_dve, job + 1)
                        out = mtmp[:, a, :] if w == 0 else merged[:, m, a * HALF:(a + 1) * HALF]
                        took(vec.tensor_tensor(out, bank(job)[:, 0:HALF], gates[:, m % 2, w, a, :], ALU.mult), job)
                vec.tensor_tensor(merged[:, m, :], merged[:, m, :], mtmp[:, :, :].rearrange("p a t -> p (a t)"),
                                  ALU.add).then_inc(merged_ready, 1)
                dve.wait_ge(merged_ready, m + 1)
            ROWS = ((g1_row, mod[:, 16:24, :]), (a2_row, scale2[:, :, :]), (b2_row, mod[:, 24:32, :]),
                    (g2_row, mod[:, 40:48, :]))

            def make_diag(n):
                src = ROWS[n // 4][1][:, 4 * (n % 2):4 * (n % 2) + 4, n // 2 % 2]
                vec.tensor_tensor(diag[:, n % 2, :].rearrange("p (k t) -> p k t", k=4), bc(ident, 1, 4), bc(src, 2, P),
                                  ALU.mult).then_inc(row_diag, 1)

            dve.wait_ge(tile_used, TILES)
            make_diag(0)
            for n in range(16):
                if n + 1 < 16:
                    make_diag(n + 1)
                job = V["row"] + n
                dve.wait_ge(for_dve, job + 1)
                took(vec.tensor_copy(ROWS[n // 4][0][:, n // 2 % 2, 512 * (n % 2):512 * (n % 2) + 512], bank(job)),
                     job)
            for c in range(CH):
                cv = 0 if c < SCH else 1
                dve.wait_ge(xp_in[c % 2], 32 * (c // 2) + (32 if c < SCH else 16))
                if c < SCH:
                    done(vec.tensor_tensor(xp[:, c % 2, 0, :], xp[:, c % 2, 0, :], xp[:, c % 2, 1, :], ALU.add))
                for half in range(2):
                    job = V["wo"] + 2 * c + half
                    cols = slice(512 * half, 512 * half + 512)
                    dve.wait_ge(for_dve, job + 1)
                    took(vec.tensor_tensor(x2[:, c, cols], bank(job), g1_row[:, cv, cols], ALU.mult), job)
                vec.tensor_tensor(x2[:, c, :], x2[:, c, :], xp[:, c % 2, 0, :], ALU.add).then_inc(x2_ready, 1)
                if c >= 1:
                    norm2(c - 1)
            norm2(CH - 1)
            def tile3(n, m=EXPERTS):
                return rt[:, n, 0:CH * m].rearrange("p (c e) -> p c e", c=CH)

            N_SC, N_SEL, N_RANK, N_GS, N_GR, N_M, N_W, N_D5, N_POS, N_CAR, N_CNT, N_OV, N_INC, N_OB, N_START, \
                N_AFTER, N_ROW, N_T1, N_T2, N_A, N_B = range(21)
            cmp1 = rcmp[:, 0, :].rearrange("p (g j k) -> p g j k", j=EPG, k=EPG)
            cmp2 = rcmp[:, 1, :].rearrange("p (g j k) -> p g j k", j=EPG, k=EPG)
            lower = con("lower").rearrange("p (j k) -> p j k", j=EPG)

            def ranks(out, vals, groups):
                other = vals.unsqueeze(2).broadcast_to((P, groups, EPG, EPG))
                own = vals.unsqueeze(3).broadcast_to((P, groups, EPG, EPG))
                c1, c2 = cmp1[:, 0:groups, :, :], cmp2[:, 0:groups, :, :]
                note(vec.tensor_tensor(c1, other, own, ALU.is_gt))
                done(vec.tensor_tensor(c2, other, own, ALU.is_equal))
                done(vec.tensor_tensor(c2, c2, bc(lower, 1, groups), ALU.mult))
                done(vec.tensor_tensor(c1, c1, c2, ALU.add))
                done(vec.tensor_reduce(out, c1, AX.X, ALU.add))

            dve.wait_ge(act_took, A["logit"] + 1)
            done(vec.tensor_tensor(tile3(N_SEL), tile3(N_SC), bc(par("router_b"), 1, CH), ALU.add))
            sel = rt[:, N_SEL, :].rearrange("p (g j) -> p g j", j=EPG)
            ranks(rt[:, N_RANK, :].rearrange("p (g j) -> p g j", j=EPG), sel, CH * EGROUPS)
            done(vec.tensor_scalar(rt[:, N_RANK, :], rt[:, N_RANK, :], 1.5, None, ALU.is_lt))
            done(vec.tensor_tensor(rt[:, N_T1, :], rt[:, N_SEL, :], rt[:, N_RANK, :], ALU.mult))
            done(vec.tensor_reduce(rt[:, N_GS, 0:20], rt[:, N_T1, :].rearrange("p (g j) -> p g j", j=EPG), AX.X, ALU.add))
            ranks(rt[:, N_GR, 0:20].rearrange("p (g j) -> p g j", j=EGROUPS),
                  rt[:, N_GS, 0:20].rearrange("p (g j) -> p g j", j=EGROUPS), CH)
            done(vec.tensor_scalar(rt[:, N_GR, 0:20], rt[:, N_GR, 0:20], 0.5, None, ALU.is_lt))
            vec.tensor_tensor(rt[:, N_M, :].rearrange("p (g j) -> p g j", j=EPG),
                              rt[:, N_RANK, :].rearrange("p (g j) -> p g j", j=EPG), bc(rt[:, N_GR, 0:20], 2, EPG),
                              ALU.mult).then_inc(sel_ready, 1)
            dve.wait_ge(sel_ready, 1)
            done(vec.tensor_tensor(rt[:, N_W, :], rt[:, N_SC, :], rt[:, N_M, :], ALU.mult))
            done(vec.tensor_reduce(rt[:, N_D5, 0:5], tile3(N_W), AX.X, ALU.add))
            done(vec.reciprocal(rt[:, N_D5, 0:5], rt[:, N_D5, 0:5]))
            done(vec.tensor_tensor(tile3(N_W), tile3(N_W), bc(rt[:, N_D5, 0:5], 2, EXPERTS), ALU.mult))
            job = V["prefix"]
            dve.wait_ge(for_dve, job + 1)
            pre = bank(job)
            note(vec.tensor_copy(rt[:, N_T2, :], pre[:, 80:160]))
            took(vec.tensor_copy(rt[:, N_POS, :], pre[:, 0:80]), job)
            settle()
            for c in range(1, CH):
                if c == 1:
                    done(vec.tensor_copy(tile3(N_CAR)[:, 1, :], tile3(N_T2)[:, 0, :]))
                else:
                    done(vec.tensor_tensor(tile3(N_CAR)[:, c, :], tile3(N_CAR)[:, c - 1, :], tile3(N_T2)[:, c - 1, :],
                                           ALU.add))
            note(vec.tensor_tensor(rt[:, N_CNT, 0:16], tile3(N_CAR)[:, CH - 1, :], tile3(N_T2)[:, CH - 1, :], ALU.add))
            done(vec.tensor_tensor(tile3(N_POS)[:, 1:, :], tile3(N_POS)[:, 1:, :], tile3(N_CAR)[:, 1:, :], ALU.add))
            cnt, ov, inc, ob, start, after = (rt[:, n, 0:16] for n in (N_CNT, N_OV, N_INC, N_OB, N_START, N_AFTER))
            done(vec.tensor_scalar(ov, cnt, float(P), None, ALU.is_gt))
            for j in range(2, CH):
                done(vec.scalar_tensor_tensor(ov, cnt, float(j * P), ov, ALU.is_gt, ALU.add))
            done(vec.tensor_tensor_scan(inc, ones[:, 0:16], ov, 0.0, ALU.mult, ALU.add))
            done(vec.tensor_tensor(ob, inc, ov, ALU.subtract))
            note(vec.tensor_tensor(start, ob, par("count")[:, 0:EXPERTS], ALU.add))
            done(vec.tensor_tensor(after, inc, par("count")[:, 1:EXPERTS + 1], ALU.add))
            done(vec.scalar_tensor_tensor(tile3(N_ROW), bc(start, 1, CH), float(P), tile3(N_POS), ALU.mult, ALU.add))
            big = float(1 << 20)
            done(vec.tensor_scalar(rt[:, N_T1, :], rt[:, N_M, :], -big, big, ALU.mult, ALU.add))
            note(vec.tensor_tensor(rt[:, N_A, :], rt[:, N_ROW, :], rt[:, N_T1, :], ALU.add))
            done(vec.tensor_tensor(rt[:, N_B, :], rt[:, N_ROW, :], rt[:, N_M, :], ALU.mult))
            note(vec.tensor_reduce(rt[:, N_D5, 0:5], tile3(N_A), AX.X, ALU.min))
            done(vec.tensor_reduce(rt[:, N_D5, 5:10], tile3(N_B), AX.X, ALU.max))
            for j, n in enumerate((N_A, N_B)):
                done(vec.tensor_tensor(tile3(n), tile3(n), bc(rt[:, N_D5, 5 * j:5 * j + 5], 2, EXPERTS), ALU.is_equal))
                done(vec.tensor_tensor(rt[:, n, :], rt[:, n, :], rt[:, N_W, :], ALU.mult))
                done(vec.tensor_reduce(rt[:, N_GS, 20 + 5 * j:25 + 5 * j], tile3(n), AX.X, ALU.add))
            note(vec.tensor_copy(rint[:, 26:36], rt[:, N_D5, 0:10]))
            own = bc(par("count")[:, 0:NBLK], 2, EXPERTS)
            r1 = rcmp[:, :, :].rearrange("p a n -> p (a n)")[:, 0:NBLK * EXPERTS].rearrange("p (j e) -> p j e", j=NBLK)
            done(vec.tensor_tensor(r1, own, bc(after, 1, NBLK), ALU.is_ge))
            done(vec.tensor_reduce(rt[:, N_T1, 0:NBLK], r1, AX.X, ALU.add))
            note(vec.tensor_copy(rint[:, 0:NBLK], rt[:, N_T1, 0:NBLK]))
            note(vec.tensor_copy(rint[:, NBLK:NBLK + 1], after[:, EXPERTS - 1:EXPERTS]))
            done(vec.tensor_scalar(rint[:, START:START + EXPERTS], start, -1.0, None, ALU.add))
            vec.nop().then_inc(route_ready, 1)
            blocks = dve.value_load(rint[0:1, 25:26], min_val=EXPERTS, max_val=NBLK)
            with dve.Fori(0, NBLK) as i:
                with dve.If(i < blocks):
                    for f in range(KF):
                        dve.wait_ge(silu_ready, i * KF + f + 1)
                        vec.tensor_tensor(act_t[:, f, :], silu[:, f % 2, :], ps[:, 2 + f % 2, 0:P], ALU.mult)\
                            .then_inc(prod_ready, 1)
                    dve.wait_ge(down_done, i * KF + KF)
                    dve.wait_ge(y_free, i + 1)
                    vec.tensor_copy(y_blk[:, 512:1024], ps[:, 5, :]).then_inc(y_copied, 1)
                dve.nop()
            w_of = rt[:, N_GS, 20:30]
            for c in range(CH):
                cv = 0 if c < SCH else 1
                dve.wait_ge(got_in[c], 32)
                done(vec.tensor_scalar(got[2 * c][:, :], got[2 * c][:, :], w_of[:, c:c + 1], None, ALU.mult))
                done(vec.scalar_tensor_tensor(got[2 * c][:, :], got[2 * c + 1][:, :], w_of[:, 5 + c:6 + c],
                                              got[2 * c][:, :], ALU.mult, ALU.add))
                done(vec.tensor_tensor(got[2 * c][:, :], got[2 * c][:, :], g2_row[:, cv, :], ALU.mult))
                vec.tensor_tensor(fin[c][:, :], got[2 * c][:, :], x2[:, c, :], ALU.add).then_inc(x3_ready, 1)
                if c >= 1:
                    final(c - 1)
            final(CH - 1)

        @block.tensor
        def _(pe):
            mm = nc.tensor.matmul

            def act_bank(job):
                if job >= 3:
                    pe.wait_ge(act_took, job - 2)

            def dve_bank(job):
                if job >= 2:
                    pe.wait_ge(dve_took, job - 1)

            owed = [0]

            def free_tiles(n=1):
                owed[0] += n

            def first(ins):
                if owed[0]:
                    ins.then_inc(tile_used, owed[0])
                    owed[0] = 0

            def tile(t):
                pe.wait_ge(tile_in[t % RING], 16 * (t // RING + 1))
                return ring[:, t % RING, :, :]

            def project(job, t, used=1):
                act_bank(job)
                w = tile(t)
                for k in range(KD):
                    for a in range(2):
                        last = mm(pair(job)[:, a, :], w[:, k, :], h_t[:, k, a * HALF:(a + 1) * HALF],
                                  start=(k == 0), stop=(k == KD - 1))
                        if k == 0 and a == 0:
                            first(last)
                last.then_inc(for_act, 1)
                free_tiles(used)

            def vectors(job, t0, count):
                dve_bank(job)
                for j in range(count):
                    last = vector_tile(job, j, t0 + j)
                last.then_inc(for_dve, 1)

            def vector_tile(job, j, t):
                w = tile(t)
                for k in range(KD):
                    last = mm(bank(job)[:, 2 * j:2 * j + P], w[:, k, :], bc(csil[:, k, :], 1, P // 2),
                              start=(k == 0), stop=(k == KD - 1))
                    if k == 0:
                        first(last)
                free_tiles()
                return last

            def head_squares(c):
                job = A["oss"] + c
                pe.wait_ge(osq_ready, c + 1)
                act_bank(job)
                nc.tensor.matmul(pair_flat(job)[:, 0, :], ones, o_sq[:, :, :].rearrange("p h t -> p (h t)"), start=True,
                                 stop=True).then_inc(for_act, 1)

            pe.wait_ge(c_ready, 1)
            vectors(V["ada1"], T_ADA1, 16)
            pe.wait_ge(const_in, 16)
            pe.wait_ge(sq_ready, 1)
            for k in range(KD):
                for a in range(2):
                    last = mm(pair(A["ss1"])[:, a, :], ones, x_sq[:, k, a * HALF:(a + 1) * HALF], start=(k == 0),
                              stop=(k == KD - 1))
                    if k == 0 and a == 0:
                        first(last)
            last.then_inc(for_act, 1)
            pe.wait_ge(h_ready, 1)
            for m in range(4):
                project(A["u"] + m, T_U + m)
            for m in range(4):
                project(A["q"] + m, T_Q + m)
            for n in range(8):
                d, ri, half = n // 4, n // 2 % 2, n % 2
                job = A["gt"] + n
                pe.wait_ge(gpre_ready, d + 1)
                act_bank(job)
                for i in range(8):
                    last = nc.tensor.transpose(pair_flat(job)[:, i // 4, (i % 4) * P:(i % 4) * P + P],
                                               gpre[d][:, ri, 8 * half + i, :, :].rearrange("p s c -> p (s c)"), ident)
                last.then_inc(for_act, 1)
            pe.wait_ge(u_loaded, 16 * BLK)
            pe.wait_ge(act_took, A["gt"] + 8)
            for n in range(8):
                d, ri, half = n // 4, n // 2 % 2, n % 2
                job = A["x"] + n
                act_bank(job)
                for i in range(8):
                    pr = 8 * half + i
                    for g2 in range(2):
                        last = mm(pair(job)[g2 * STATE:(g2 + 1) * STATE, i // 4, (i % 4) * NB:(i % 4 + 1) * NB],
                                  gt[:, d, ri, pr, g2 * STATE:(g2 + 1) * STATE], uf[:, 2 * pr + g2, :], start=True,
                                  stop=True)
                last.then_inc(for_act, 1)
            for m in range(4):
                project(A["ff"] + m, T_FF + m)
            for m in range(4):
                project(A["fb"] + m, T_FB + m)
            for m in range(4):
                tile(T_V + m)
            slots = [(T_V + m) % RING for m in range(4)]
            for c in range(CH):
                job = A["v"] + c
                act_bank(job)
                for m in range(4):
                    for k in range(KD):
                        last = mm(pair_flat(job)[:, 0, m * P:(m + 1) * P], h_t[:, k, c * P:(c + 1) * P],
                                  ring[:, slots[m], k, :], start=(k == 0), stop=(k == KD - 1))
                        if k == 0:
                            first(last)
                last.then_inc(for_act, 1)
            free_tiles(4)
            pe.wait_ge(m_ready, 2)
            for n in range(4):
                job = V["k"] + n
                dve_bank(job)
                g2 = n % 2
                for jj in range(2):
                    j = 4 * (n // 2) + 2 * jj + g2
                    rows = slice(g2 * STATE, (g2 + 1) * STATE)
                    for d in range(2):
                        for r in range(4):
                            pr = 4 * (j // 2) + r
                            for ri in range(2):
                                last = mm(bank(job)[32 * r:32 * r + 32, (2 * jj + d) * P:(2 * jj + d + 1) * P],
                                          bbar[rows, ri, d, pr * GC:pr * GC + 32],
                                          m_lhs[rows, d, ri, pr, d:d + BLK, :].rearrange("p t c -> p (t c)"),
                                          start=(ri == 0), stop=(ri == 1))
                                if ri == 0:
                                    first(last)
                last.then_inc(for_dve, 1)
            vectors(V["ada2"], T_ADA2, ADA_MID - ADA_Y)
            pe.wait_ge(w_loaded_act, 16 * 24)
            pe.wait_ge(w_loaded, 16 * 8)
            pe.wait_ge(scan_done, 1)
            dve_bank(V["ada_y"])
            ada_y = 0
            for n in range(4):
                job = A["y"] + n
                act_bank(job)
                for gg in range(8):
                    pr, g2 = 4 * n + gg % 4, gg // 4
                    r, j = pr % 4, 2 * (pr // 4) + g2
                    last = mm(pair(job)[:, g2, (gg % 4) * NB:(gg % 4 + 1) * NB], wt[:, r, j, :], uf[:, 2 * pr + g2, :],
                              start=(gg % 4 == 0), stop=False, skip_group_check=True)
                    if gg == 0:
                        first(last)
                for gg in range(8):
                    pr, g2 = 4 * n + gg % 4, gg // 4
                    rows = slice(g2 * STATE, (g2 + 1) * STATE)
                    out = pair(job)[:, g2, (gg % 4) * NB:(gg % 4 + 1) * NB]
                    for ri in range(2):
                        for d in range(2):
                            lhs = m_lhs[rows, d, ri, pr, 1 - d:1 - d + BLK, :].rearrange("p t c -> p (t c)")
                            col = d * 32 + ri * PAIRS + pr
                            if d == 0:
                                mm(out, lhs, xh[rows, 0:NB, col], start=False, stop=False, skip_group_check=True)
                            else:
                                mm(out[:, 0:SB], lhs, xh[rows, SB - 1::-1, col], start=False, stop=False,
                                   skip_group_check=True)
                                last = mm(out[:, SB:NB], lhs, xh[rows, NB - 1:SB - 1:-1, col], start=False,
                                          stop=(ri == 1), skip_group_check=True)
                    if gg == 7:
                        last.then_inc(for_act, 1)
                    if (n * 8 + gg + 1) * ADA_Y // 32 > ada_y:
                        last = vector_tile(V["ada_y"], ada_y, T_ADA2 + ADA_MID - ADA_Y + ada_y)
                        ada_y += 1
            last.then_inc(for_dve, 1)
            pe.wait_ge(g_loaded, 16)
            for m in range(4):
                job = A["glu"] + m
                act_bank(job)
                w = tile(T_GLU + m // 2)
                for k in range(4):
                    for a in range(2):
                        last = mm(pair(job)[:, a, :], w[:, 4 * (m % 2) + k, :], g_t[:, k, a * HALF:(a + 1) * HALF],
                                  start=(k == 0), stop=(k == 3))
                        if k == 0 and a == 0:
                            first(last)
                last.then_inc(for_act, 1)
                free_tiles(m % 2)
            for d in range(2):
                pe.wait_ge(kd_ready, d + 1)
                for c in range(CH):
                    job = A["kt"] + d * CH + c
                    act_bank(job)
                    for h in range(HEADS):
                        last = nc.tensor.transpose(pair_flat(job)[:, 0, h * P:(h + 1) * P],
                                                   node_x[d][:, h, c * P:(c + 1) * P], ident)
                        if h == 0:
                            first(last)
                    last.then_inc(for_act, 1)
                pe.wait_ge(act_took, A["kt"] + (d + 1) * CH)
                for n, c in enumerate((0, 1, 2, SCH) if d == 0 else (3, 2, 1, SCH)):
                    job = V["kv"] + 4 * d + n
                    dve_bank(job)
                    for h in range(HEADS):
                        last = mm(bank(job)[:, h * P:(h + 1) * P], kd_t[:, c, h, :], v[:, c, h * P:(h + 1) * P],
                                  start=True, stop=True)
                    last.then_inc(for_dve, 1)
            pe.wait_ge(diag_ready, 1)
            for c in range(CH):
                job = V["diag"] + c
                dve_bank(job)
                for h in range(HEADS):
                    last = mm(bank(job)[:, h * P:(h + 1) * P], node_x[1][:, h, c * P:(c + 1) * P],
                              q[:, h, c * P:(c + 1) * P], start=True, stop=True)
                last.then_inc(for_dve, 1)
            for s in range(len(STEPS)):
                pe.wait_ge(node_ready, s + 1)
                x = node_x[s % 2]
                for c in range(CH):
                    job = V["node"] + s * (CH + 1) + c
                    dve_bank(job)
                    for h in range(HEADS):
                        both = x[:, h, c * P:(c + 1) * P]
                        last = mm(bank(job)[:, h * P:(h + 1) * P], both, both, start=True, stop=True)
                        if c == 0 and h == 0:
                            first(last)
                    last.then_inc(for_dve, 1)
                vectors(V["node"] + s * (CH + 1) + CH, T_ADA3 - 16 - ADA_MID + ADA_AT[s], ADA_AT[s + 1] - ADA_AT[s])
            for m in range(4):
                project(A["g"] + m, T_G + m)
            pe.wait_ge(att_ready, 1)
            pe.wait_ge(qd_ready, 2)
            pe.wait_ge(states_ready, 1)
            for c in range(CH):
                job = V["o"] + c
                dve_bank(job)
                for h in range(HEADS):
                    out = bank(job)[:, h * P:(h + 1) * P]
                    last = mm(out, v[:, c, h * P:(h + 1) * P], att[:, c, h, :], start=True, stop=(c == SCH))
                    if c == 0 and h == 0:
                        first(last)
                    if c < SCH:
                        for d in range(2):
                            last = mm(out, st[:, d, c, h, :], node_x[d][:, h, c * P:(c + 1) * P], start=False,
                                      stop=(d == 1))
                last.then_inc(for_dve, 1)
                if c >= 1:
                    head_squares(c - 1)
            head_squares(CH - 1)
            pe.wait_ge(y_s5_ready, 1)
            for m in range(KD):
                for w in range(2):
                    project(A["gate"] + 2 * m + w, T_MERGE + 3 * m + 2 * w, used=1 - w)
                    if m == 0 and w == 0:
                        pe.wait_ge(y_hg_ready, CH)
                    br = tile(T_MERGE + 3 * m + 1)
                    y = y_s5 if w == 0 else y_hg
                    for a in range(2):
                        job = V["br"] + 4 * m + 2 * w + a
                        dve_bank(job)
                        for k in range(4):
                            last = mm(bank(job)[:, 0:HALF], br[:, 4 * w + k, :], y[:, k, a * HALF:(a + 1) * HALF],
                                      start=(k == 0), stop=(k == 3))
                            if k == 0:
                                first(last)
                        last.then_inc(for_dve, 1)
                    free_tiles(2 * w)
            pe.wait_ge(for_dve, V["row"])
            pe.nop().then_inc(tile_used, owed[0])
            for n in range(16):
                job = V["row"] + n
                pe.wait_ge(row_diag, n + 1)
                dve_bank(job)
                mm(bank(job), ones, diag[:, n % 2, :], start=True, stop=True).then_inc(for_dve, 1)
            pe.wait_ge(wo_in, 16)
            pe.wait_ge(merged_ready, KD)
            for c in range(CH):
                for half in range(2):
                    job = V["wo"] + 2 * c + half
                    dve_bank(job)
                    for k in range(KD):
                        last = mm(bank(job), merged[:, k, c * P:(c + 1) * P], wo[:, k, 512 * half:512 * half + 512],
                                  start=(k == 0), stop=(k == KD - 1))
                    last.then_inc(for_dve, 1)
            for c in range(CH):
                job = A["h2t"] + c
                pe.wait_ge(h2_ready, c + 1)
                act_bank(job)
                for k in range(KD):
                    last = nc.tensor.transpose(pair_flat(job)[:, k // 4, (k % 4) * P:(k % 4 + 1) * P],
                                               h2[:, c, k * P:(k + 1) * P], ident)
                last.then_inc(for_act, 1)
            pe.wait_ge(rw_in, 16)
            job = A["logit"]
            act_bank(job)
            pe.wait_ge(act_took, A["h2t"] + CH)
            for c in range(CH):
                for k in range(KD):
                    last = mm(pair_flat(job)[:, 0, c * EXPERTS:(c + 1) * EXPERTS], h2_t[:, k, c * P:(c + 1) * P],
                              rw[:, k, :], start=(k == 0), stop=(k == KD - 1))
            last.then_inc(for_act, 1)
            pe.wait_ge(sel_ready, 1)
            job = V["prefix"]
            dve_bank(job)
            mm(bank(job)[:, 0:80], con("before"), rt[:, 5, :], start=True, stop=True)
            mm(bank(job)[:, 80:160], ones, rt[:, 5, :], start=True, stop=True).then_inc(for_dve, 1)
            pe.wait_ge(route_ready, 1)
            blocks = pe.value_load(rint[0:1, 25:26], min_val=EXPERTS, max_val=NBLK)

            def transpose_x():
                for k in range(KD):
                    last = nc.tensor.transpose(ps[:, 6 + k // 4, (k % 4) * P:(k % 4 + 1) * P],
                                               x_blk[:, k * P:(k + 1) * P], ident)
                last.then_inc(xt_done, 1)

            pe.wait_ge(x_blk_in, 16)
            transpose_x()
            with pe.Fori(0, NBLK) as i:
                with pe.If(i < blocks):
                    e = pe.value_load(rint[0:1, bass.ds(i, 1)], min_val=0, max_val=EXPERTS - 1)
                    pe.wait_ge(xt_copied, i + 1)

                    def down(f):
                        pe.wait_ge(prod_ready, i * KF + f + 1)
                        pe.wait_ge(dn_in[f], e * 16 + 16)
                        if f == 0:
                            pe.wait_ge(y_copied, i * 2 + 1)
                        for half in range(2):
                            last = mm(ps[:, 4 + half, :], act_t[:, f, :],
                                      w_slot[3 * f + 2][:, 4 * half:4 * half + 4, :].rearrange("p k c -> p (k c)"),
                                      start=(f == 0), stop=(f == KF - 1))
                        last.then_inc(down_done, 1)

                    for f in range(KF):
                        pe.wait_ge(gu_in[f], e * 32 + 32)
                        if f >= 2:
                            pe.wait_ge(prod_ready, i * KF + f - 1)
                        for w in range(2):
                            for k in range(KD):
                                last = mm(ps[:, 2 * w + f % 2, 0:P], w_slot[3 * f + w][:, k, :], x_blk_t[:, k, :],
                                          start=(k == 0), stop=(k == KD - 1))
                        last.then_inc(gu_done, 1)
                        if f == KF - 1:
                            pe.wait_ge(x_blk_in, i * 16 + 32)
                            transpose_x()
                        if f >= 1:
                            down(f - 1)
                    down(KF - 1)
                pe.nop()



def _tiles(w, n):
    k = w.shape[0] // P
    return w.reshape(k, P, n, P).transpose(2, 1, 0, 3)


def _constants():
    cst = np.zeros((P, CONST_COLS), np.float32)
    cst[:, 0:128] = np.eye(P)
    cst[:, 128:256] = 1.0
    cst[:, 256:384] = np.triu(np.ones((P, P)), 1)
    t = np.arange(TOK)
    cst[:, 384:1024] = (t % P != 0)
    cst[:, 1024:1664] = (t % P != P - 1)
    cst[:, 1664:1680] = np.tril(np.ones((EPG, EPG)), -1).reshape(-1)
    cst[:, 1680] = EPS
    masks = np.zeros((P, 2 * LEVELS, P), np.float32)
    s, t = np.arange(P)[:, None], np.arange(P)[None, :]
    for l in range(LEVELS):
        half = (P // 2) >> l
        left = (s // (2 * half) == t // (2 * half)) & (s // half % 2 == 0) & (t // half % 2 == 1)
        masks[:, l] = left
        masks[:, LEVELS + l] = left.T
    return cst, masks


def _positions():
    quarter = D // 4
    grid_w = 64
    omega = (np.float32(1.0) / (np.float32(10000.0) ** (np.arange(quarter, dtype=np.float32) / np.float32(quarter))))

    def embed(n):
        ang = np.arange(n, dtype=np.float32)[:, None] * omega[None, :].astype(np.float32)
        return np.concatenate([np.sin(ang), np.cos(ang)], axis=-1).astype(np.float32)

    row, col = embed(SAMPLE // grid_w), embed(grid_w)
    full = np.concatenate([np.repeat(row, grid_w, axis=0), np.tile(col, (SAMPLE // grid_w, 1))], axis=-1)
    return row, col, full


def kernel(**inputs):
    import concourse.bacc as bacc
    from concourse.bass_utils import run_bass_kernel_spmd

    a = {k: np.asarray(x) for k, x in inputs.items()}
    x_all = np.concatenate([a["x_sample"][0], a["x_prompt"][0]], axis=0)
    row, col, full = _positions()
    cst, masks = _constants()

    def by_state(x):
        return x.reshape(2, PAIRS, 2, STATE).transpose(2, 3, 0, 1).reshape(P, 32)

    def by_pair(x):
        return x.reshape(PAIRS, 2, STATE, GC).transpose(1, 2, 0, 3).reshape(P, PAIRS * GC)

    small = np.zeros((P, SMALL_COLS), np.float32)

    def fill(name, x):
        at, n = SMALL[name]
        small[:, at:at + n] = x

    fill("lam_re", by_state(a["s5_lam_re"][0]))
    fill("lam_im", by_state(a["s5_lam_im"][0]))
    fill("log_step", by_state(np.broadcast_to(a["s5_log_step"][0][:, :, None], (2, GROUPS, STATE))))
    fill("b_re", by_pair(a["s5_b_re"][0]))
    fill("b_im", by_pair(a["s5_b_im"][0]))
    fill("c_re", by_pair(a["s5_c_re"][0].transpose(0, 2, 1)))
    fill("c_im", by_pair(a["s5_c_im"][0].transpose(0, 2, 1)))
    h0 = np.stack([by_state(a["state_s5_re"][0, 0]).reshape(P, 2, PAIRS),
                   by_state(a["state_s5_im"][0, 0]).reshape(P, 2, PAIRS)], axis=2)
    fill("h0", h0.reshape(P, SLOT))
    cvec = np.stack([a["c"][0], a["c_ctx"]], axis=1)
    fill("cvec", cvec.reshape(KD, P, 2).transpose(1, 0, 2).reshape(P, 16))
    fill("b_ada", a["b_ada"][0].reshape(48, P).T)
    fill("norm1", a["norm1_w"][0].reshape(KD, P).T)
    fill("norm2", a["norm2_w"][0].reshape(KD, P).T)
    fill("lb_logits", a["hg_lb_logits"][0].reshape(8, P).T)
    fill("hg_norm", a["hg_norm_w"][0].reshape(4, P).T)
    fill("b_glu", a["s5_b_glu"][0].reshape(4, P).T)
    sd = np.zeros((4, 32, 8), np.float32)
    sd[:, :GC, :] = a["s5_d"][0].reshape(4, 4, 2, GC).transpose(1, 3, 0, 2).reshape(4, GC, 8)
    fill("s5_d", sd.reshape(P, 8))
    fill("router_b", a["router_b"][None, :])
    fill("pos_row", row.T.reshape(4, P, 8).transpose(1, 0, 2).reshape(P, 32))
    fill("pos_col", col.T.reshape(4, P, 64).transpose(1, 0, 2).reshape(P, 256))
    fill("id16", np.tile(np.concatenate([np.eye(GC), np.zeros((GC, GC))]), (4, 1)))
    fill("count", np.arange(32)[None, :])

    ada = _tiles(a["w_ada"][0], 48)
    w_in = _tiles(a["w_in"][0], 40)
    glu = _tiles(a["s5_w_glu"][0], 4)
    glu = glu.reshape(2, 2, P, 4, P).transpose(0, 2, 1, 3, 4).reshape(2, P, KD, P)
    br = np.concatenate([_tiles(a["w_br_s5"][0], KD), _tiles(a["w_br_hg"][0], KD)], axis=2)
    merge = np.stack([w_in[24:32], br, w_in[32:40]], axis=1).reshape(3 * KD, P, KD, P)
    stream = np.concatenate([ada[0:16], w_in[0:20], ada[16:16 + ADA_MID], glu, ada[16 + ADA_MID:48], w_in[20:24], merge],
                            axis=0)

    def expert_cols(w):
        return np.ascontiguousarray(w.reshape(EXPERTS, KD, P, KF, P).transpose(0, 3, 2, 1, 4))

    ins = {
        "x_t": x_all.T.reshape(KD, P, TOK).transpose(1, 0, 2),
        "x_rows": x_all.reshape(CH, P, D),
        "pos_rows": full.reshape(SCH, P, D),
        "small": small,
        "const": cst,
        "masks": masks,
        "stream": stream,
        "w_out": a["w_out"][0].reshape(KD, P, D).transpose(1, 0, 2),
        "norm_f": a["norm_f_w"].reshape(1, D),
        "hg_state": a["state_hg"][0, 0],
        "router_w": a["router_w"].reshape(KD, P, EXPERTS).transpose(1, 0, 2),
        "w_gate": expert_cols(a["moe_w_gate"][0]),
        "w_up": expert_cols(a["moe_w_up"][0]),
        "w_down": a["moe_w_down"][0].reshape(EXPERTS, KF, P, KD, P),
    }
    outs = {"y_rows": (CH, P, D), "s5_new": (P, SLOT), "hg_new": (2, HEADS, P, P)}
    nc = bacc.Bacc("TRN2", target_bir_lowering=False, num_devices=1)
    arrays, args = {}, []
    for name, x in ins.items():
        x = np.ascontiguousarray(x)
        arrays["in_" + name] = x
        args.append(nc.dram_tensor("in_" + name, x.shape, mybir.dt.from_np(x.dtype), kind="ExternalInput").ap())
    for name, shape in outs.items():
        args.append(nc.dram_tensor("out_" + name, shape, F32, kind="ExternalOutput").ap())
    hybrid_step(nc, *args)
    r = run_bass_kernel_spmd(nc, [arrays], core_ids=[0])
    y = np.asarray(r.results[0]["out_y_rows"]).reshape(TOK, D)
    s5 = np.asarray(r.results[0]["out_s5_new"]).reshape(2, STATE, 2, 2, PAIRS)
    s5 = s5.transpose(3, 2, 4, 0, 1).reshape(2, 2, GROUPS, STATE)
    hg = np.asarray(r.results[0]["out_hg_new"])
    return (y[SAMPLE:][None], y[:SAMPLE][None], s5[0][None, None], s5[1][None, None], hg[None, None])
```
